# Optimizing a Trainium2 kernel written in Bass

```python
import math
import jax
import jax.numpy as jnp
from jax import lax
import numpy as np

D_MODEL = 1024
BATCH = 1
SEQ = 256
DEPTH = 1
DEC_BATCH = 8
DEC_SEQ = 1
PAST_LEN = 2048
PAGE_SIZE = 128

N_META = 16
H_A = 4
DK_A = 128
DV_A = 128
D_A_K = H_A * DK_A
D_A_V = H_A * DV_A
H_B = 4
DK_B = 128
DV_B = 128
D_B_K = H_B * DK_B
D_B_V = H_B * DV_B
CONV_W = 4
D_CONV = 2 * D_B_K + D_B_V
CHUNK = 64
D_IN = 2 * D_A_K + 2 * D_A_V + D_CONV + 2 * H_B + D_B_V + 2 * D_MODEL
N_EXPERTS = 32
TOP_K = 4
D_FF = D_MODEL
SWIGLU_LIMIT = 7.0
SWIGLU_ALPHA = 1.702
MOE_BLOCK = 128
RMS_EPS = 1e-6
L2_EPS = 1e-6

kernel_name = "hgrn2_gdn_parallel_moe_step"

def _rmsnorm(x, w):
    xf = x.astype(jnp.float32)
    y = xf * lax.rsqrt(jnp.mean(xf * xf, axis=-1, keepdims=True) + RMS_EPS)
    return (y * w.astype(jnp.float32)).astype(x.dtype)

def _l2norm(x):
    return x * lax.rsqrt(jnp.sum(x * x, axis=-1, keepdims=True) + L2_EPS)

def _split_cols(p):
    sizes = (D_A_K, D_A_K, D_A_V, D_A_V, D_CONV, H_B, H_B, D_B_V, D_MODEL, D_MODEL)
    idx = [int(i) for i in np.cumsum(sizes)[:-1]]
    return jnp.split(p, idx, axis=-1)

def _to_chunks(x):
    B, Lp, H = x.shape[:3]
    x = x.reshape((B, Lp // CHUNK, CHUNK, H) + x.shape[3:])
    return jnp.moveaxis(x, (1, 3), (0, 2))

def _from_chunks(x):
    x = jnp.moveaxis(x, (0, 2), (1, 3))
    B, N, C, H = x.shape[:4]
    return x.reshape((B, N * C, H) + x.shape[4:])

def _hgrn2_chunked(S0, q, k, v, log_f):
    qc, kc, vc, lfc = _to_chunks(q), _to_chunks(k), _to_chunks(v), _to_chunks(log_f)
    bcum = jnp.cumsum(lfc, axis=3)
    causal = jnp.tril(jnp.ones((CHUNK, CHUNK), dtype=bool))

    def step(S, xs):
        q_n, k_n, v_n, b_n = xs
        diff = b_n[:, :, :, None, :] - b_n[:, :, None, :, :]
        decay = jnp.exp(jnp.where(causal[:, :, None], diff, -jnp.inf))
        scores = jnp.einsum('bhtk,bhtsk->bhts', q_n, k_n[:, :, None] * decay)
        o = jnp.einsum('bhts,bhsv->bhtv', scores, v_n)
        o = o + jnp.einsum('bhtk,bhkv->bhtv', q_n * jnp.exp(b_n), S)
        b_last = b_n[:, :, -1]
        S = jnp.exp(b_last)[..., None] * S + jnp.einsum(
            'bhsk,bhsv->bhkv', k_n * jnp.exp(b_last[:, :, None] - b_n), v_n)
        return S, o

    S, o = lax.scan(step, S0, (qc, kc, vc, bcum))
    return _from_chunks(o), S

def _hgrn2_recurrent(S0, q, k, v, log_f):
    def step(S, xs):
        q_t, k_t, v_t, lf_t = xs
        S = jnp.exp(lf_t)[..., None] * S + k_t[..., None] * v_t[..., None, :]
        return S, jnp.einsum('bhk,bhkv->bhv', q_t, S)

    S, o = lax.scan(step, S0, tuple(jnp.moveaxis(a, 1, 0) for a in (q, k, v, log_f)))
    return jnp.moveaxis(o, 0, 1), S

def _gdn_chunked(S0, q, k, v, beta, g):
    qc, kc, vc = _to_chunks(q), _to_chunks(k), _to_chunks(v)
    bc, gc = _to_chunks(beta), _to_chunks(g)
    G = jnp.cumsum(gc, axis=-1)
    causal = jnp.tril(jnp.ones((CHUNK, CHUNK), dtype=bool))
    strict = jnp.tril(jnp.ones((CHUNK, CHUNK), dtype=bool), -1)
    L_dec = jnp.exp(jnp.where(causal, G[..., :, None] - G[..., None, :], -jnp.inf))
    kk = jnp.einsum('nbhtk,nbhsk->nbhts', kc, kc)
    M = jnp.where(strict, bc[..., :, None] * kk * L_dec, 0.0)
    a_mat = jnp.eye(CHUNK, dtype=M.dtype) + M
    rhs = jnp.concatenate([vc * bc[..., None], kc * (bc * jnp.exp(G))[..., None]], axis=-1)
    sol = lax.linalg.triangular_solve(a_mat, rhs, left_side=True, lower=True, unit_diagonal=True)
    U, W = sol[..., :DV_B], sol[..., DV_B:]
    A_qk = jnp.einsum('nbhtk,nbhsk->nbhts', qc, kc) * L_dec
    q_dec = qc * jnp.exp(G)[..., None]
    k_dec = kc * jnp.exp(G[..., -1:] - G)[..., None]
    g_last = jnp.exp(G[..., -1])

    def step(S, xs):
        U_n, W_n, A_n, qd_n, kd_n, gl_n = xs
        v_new = U_n - jnp.einsum('bhtk,bhkv->bhtv', W_n, S)
        o = jnp.einsum('bhtk,bhkv->bhtv', qd_n, S) + jnp.einsum('bhts,bhsv->bhtv', A_n, v_new)
        S = gl_n[..., None, None] * S + jnp.einsum('bhsk,bhsv->bhkv', kd_n, v_new)
        return S, o

    S, o = lax.scan(step, S0, (U, W, A_qk, q_dec, k_dec, g_last))
    return _from_chunks(o), S

def _gdn_recurrent(S0, q, k, v, beta, g):
    def step(S, xs):
        q_t, k_t, v_t, b_t, g_t = xs
        S = jnp.exp(g_t)[..., None, None] * S
        delta = b_t[..., None] * (v_t - jnp.einsum('bhk,bhkv->bhv', k_t, S))
        S = S + k_t[..., None] * delta[..., None, :]
        return S, jnp.einsum('bhk,bhkv->bhv', q_t, S)

    S, o = lax.scan(step, S0, tuple(jnp.moveaxis(a, 1, 0) for a in (q, k, v, beta, g)))
    return jnp.moveaxis(o, 0, 1), S

def _token_mixer(h, S_a, S_b, conv_buf, lb, w_in, conv_w, a_log, dt_bias,
                 hgrn_norm_w, gdn_norm_w, w_oa, w_ob, w_out, chunked):
    f32 = jnp.float32
    B, L, _ = h.shape
    p = jnp.einsum('bld,de->ble', h, w_in)
    q_a, f_a, i_a, g_a, qkv_b, a_b, b_b, z_b, gate_a, gate_b = _split_cols(p)
    ff = f_a.astype(f32)
    q_hg = (jax.nn.silu(q_a.astype(f32)) * DK_A ** -0.5).reshape(B, L, H_A, DK_A)
    log_f = jnp.log(lb + (1.0 - lb) * jax.nn.sigmoid(ff)).reshape(B, L, H_A, DK_A)
    k_hg = ((1.0 - lb) * jax.nn.sigmoid(-ff)).reshape(B, L, H_A, DK_A)
    v_hg = i_a.astype(f32).reshape(B, L, H_A, DV_A)
    x_ext = jnp.concatenate([conv_buf.astype(qkv_b.dtype), qkv_b], axis=1)
    new_buf = x_ext[:, L:]
    conv = sum(x_ext[:, j:j + L] * conv_w[j] for j in range(CONV_W))
    qkv = jax.nn.silu(conv.astype(f32))
    q_d, k_d, v_d = jnp.split(qkv, [D_B_K, 2 * D_B_K], axis=-1)
    q_gd = _l2norm(q_d.reshape(B, L, H_B, DK_B)) * DK_B ** -0.5
    k_gd = _l2norm(k_d.reshape(B, L, H_B, DK_B))
    v_gd = v_d.reshape(B, L, H_B, DV_B)
    beta = jax.nn.sigmoid(b_b.astype(f32))
    g_gd = -jnp.exp(a_log.astype(f32)) * jax.nn.softplus(a_b.astype(f32) + dt_bias.astype(f32))
    if chunked:
        n_pad = (-L) % CHUNK
        pad = lambda t: jnp.pad(t, [(0, 0), (n_pad, 0)] + [(0, 0)] * (t.ndim - 2))
        o_a, S_a = _hgrn2_chunked(S_a, pad(q_hg), pad(k_hg), pad(v_hg), pad(log_f))
        o_b, S_b = _gdn_chunked(S_b, pad(q_gd), pad(k_gd), pad(v_gd), pad(beta), pad(g_gd))
        o_a, o_b = o_a[:, n_pad:], o_b[:, n_pad:]
    else:
        o_a, S_a = _hgrn2_recurrent(S_a, q_hg, k_hg, v_hg, log_f)
        o_b, S_b = _gdn_recurrent(S_b, q_gd, k_gd, v_gd, beta, g_gd)
    ya = (_rmsnorm(o_a, hgrn_norm_w) * jax.nn.silu(g_a.astype(f32).reshape(B, L, H_A, DV_A))).reshape(B, L, D_A_V)
    yb = (_rmsnorm(o_b, gdn_norm_w) * jax.nn.silu(z_b.astype(f32).reshape(B, L, H_B, DV_B))).reshape(B, L, D_B_V)
    merged = (jax.nn.sigmoid(gate_a.astype(f32)) * jnp.einsum('blc,cd->bld', ya, w_oa)
              + jax.nn.sigmoid(gate_b.astype(f32)) * jnp.einsum('blc,cd->bld', yb, w_ob))
    mix = jnp.einsum('bld,de->ble', merged, w_out)
    return mix.astype(h.dtype), S_a, S_b, new_buf

def _moe(x, w_router, b_router, w_gu, b_gu, w_down, b_down):
    f32 = jnp.float32
    B, L, D = x.shape
    T = B * L
    xt = x.reshape(T, D)
    logits = jnp.einsum('td,de->te', xt, w_router).astype(f32) + b_router.astype(f32)
    top_val, top_idx = lax.top_k(logits, TOP_K)
    gates = jax.nn.softmax(top_val, axis=-1)
    A = T * TOP_K
    e_flat = top_idx.reshape(A)
    tok_flat = jnp.arange(A, dtype=jnp.int32) // TOP_K
    g_flat = gates.reshape(A)
    order = jnp.argsort(e_flat)
    e_sorted = e_flat[order]
    counts = jnp.bincount(e_flat, length=N_EXPERTS)
    padded = (counts + MOE_BLOCK - 1) // MOE_BLOCK * MOE_BLOCK
    pad_end = jnp.cumsum(padded)
    pad_start = pad_end - padded
    start = jnp.cumsum(counts) - counts
    dest = pad_start[e_sorted] + jnp.arange(A, dtype=jnp.int32) - start[e_sorted]
    n_blocks = -(-A // MOE_BLOCK) + N_EXPERTS
    P = n_blocks * MOE_BLOCK
    row_tok = jnp.full((P,), T, jnp.int32).at[dest].set(tok_flat[order])
    row_gate = jnp.zeros((P,), f32).at[dest].set(g_flat[order])
    block_expert = jnp.minimum(
        jnp.searchsorted(pad_end, jnp.arange(n_blocks) * MOE_BLOCK, side='right'), N_EXPERTS - 1)
    x_rows = jnp.concatenate([xt, jnp.zeros((1, D), xt.dtype)], axis=0)[row_tok]
    x_rows = x_rows.reshape(n_blocks, MOE_BLOCK, D)

    def expert_block(args):
        xb, e = args
        gu = xb @ w_gu[e] + b_gu[e]
        gate, up = gu[:, :D_FF], gu[:, D_FF:]
        gate = jnp.minimum(gate, SWIGLU_LIMIT)
        up = jnp.clip(up, -SWIGLU_LIMIT, SWIGLU_LIMIT)
        hmid = (up + 1.0) * gate * jax.nn.sigmoid(SWIGLU_ALPHA * gate)
        return hmid @ w_down[e] + b_down[e]

    y_rows = lax.map(expert_block, (x_rows, block_expert)).reshape(P, D)
    y = jnp.zeros((T + 1, D), f32).at[row_tok].add(y_rows.astype(f32) * row_gate[:, None])
    return y[:T].reshape(B, L, D).astype(x.dtype)

def setup_inputs(seed: int = 0) -> dict:
    key = jax.random.key(seed)
    ks = jax.random.split(key, 24)
    f32 = jnp.float32
    nrm = lambda k, shape, s: jax.random.normal(k, shape, f32) * s
    x_prompt = nrm(ks[0], (BATCH, SEQ, D_MODEL), 1.0)
    x_sample = nrm(ks[1], (DEC_BATCH, DEC_SEQ, D_MODEL), 1.0)
    state_hgrn = nrm(ks[2], (DEPTH, DEC_BATCH, H_A, DK_A, DV_A), 0.5)
    state_gdn = nrm(ks[3], (DEPTH, DEC_BATCH, H_B, DK_B, DV_B), 0.1)
    state_conv = nrm(ks[4], (DEPTH, DEC_BATCH, CONV_W - 1, D_CONV), 1.0)
    meta_tokens = nrm(ks[5], (N_META, D_MODEL), 1.0)
    lb_param = nrm(ks[6], (DEPTH + 1, D_A_K), 0.1)
    norm_mix = 1.0 + nrm(ks[7], (DEPTH, D_MODEL), 0.01)
    w_in = nrm(ks[8], (DEPTH, D_MODEL, D_IN), D_MODEL ** -0.5)
    conv_w = nrm(ks[9], (DEPTH, CONV_W, D_CONV), CONV_W ** -0.5)
    a_log = jnp.log(jax.random.uniform(ks[10], (DEPTH, H_B), f32, 1.0, 16.0))
    dt = jnp.exp(jax.random.uniform(ks[11], (DEPTH, H_B), f32, math.log(1e-3), math.log(1e-1)))
    dt_bias = dt + jnp.log(-jnp.expm1(-dt))
    hgrn_norm_w = 1.0 + nrm(ks[12], (DEPTH, DV_A), 0.01)
    gdn_norm_w = 1.0 + nrm(ks[13], (DEPTH, DV_B), 0.01)
    w_oa = nrm(ks[14], (DEPTH, D_A_V, D_MODEL), D_A_V ** -0.5)
    w_ob = nrm(ks[15], (DEPTH, D_B_V, D_MODEL), D_B_V ** -0.5)
    w_out = nrm(ks[16], (DEPTH, D_MODEL, D_MODEL), D_MODEL ** -0.5)
    norm_ffn = 1.0 + nrm(ks[17], (DEPTH, D_MODEL), 0.01)
    w_router = nrm(ks[18], (DEPTH, D_MODEL, N_EXPERTS), D_MODEL ** -0.5)
    b_router = nrm(ks[19], (DEPTH, N_EXPERTS), 0.01)
    w_gu = nrm(ks[20], (DEPTH, N_EXPERTS, D_MODEL, 2 * D_FF), D_MODEL ** -0.5)
    b_gu = nrm(ks[21], (DEPTH, N_EXPERTS, 2 * D_FF), 0.01)
    w_down = nrm(ks[22], (DEPTH, N_EXPERTS, D_FF, D_MODEL), D_FF ** -0.5)
    b_down = nrm(ks[23], (DEPTH, N_EXPERTS, D_MODEL), 0.01)
    norm_final = 1.0 + nrm(jax.random.fold_in(key, 99), (D_MODEL,), 0.01)
    return {"x_prompt": x_prompt, "x_sample": x_sample, "state_hgrn": state_hgrn,
            "state_gdn": state_gdn, "state_conv": state_conv, "meta_tokens": meta_tokens,
            "lb_param": lb_param, "norm_mix": norm_mix, "w_in": w_in, "conv_w": conv_w,
            "a_log": a_log, "dt_bias": dt_bias, "hgrn_norm_w": hgrn_norm_w,
            "gdn_norm_w": gdn_norm_w, "w_oa": w_oa, "w_ob": w_ob, "w_out": w_out,
            "norm_ffn": norm_ffn, "w_router": w_router, "b_router": b_router,
            "w_gu": w_gu, "b_gu": b_gu, "w_down": w_down, "b_down": b_down,
            "norm_final": norm_final}

def reference(x_prompt, x_sample, state_hgrn, state_gdn, state_conv, meta_tokens, lb_param,
              norm_mix, w_in, conv_w, a_log, dt_bias, hgrn_norm_w, gdn_norm_w, w_oa, w_ob,
              w_out, norm_ffn, w_router, b_router, w_gu, b_gu, w_down, b_down, norm_final):
    f32 = jnp.float32
    B = x_prompt.shape[0]
    meta = jnp.broadcast_to(meta_tokens.astype(x_prompt.dtype)[None], (B, N_META, D_MODEL))
    xp = jnp.concatenate([meta, x_prompt], axis=1)
    xs = x_sample
    lower_bounds = jnp.cumsum(jax.nn.softmax(lb_param.astype(f32), axis=0), axis=0)
    hp_list, gp_list, cp_list, hs_list, gs_list, cs_list = [], [], [], [], [], []
    for l in range(DEPTH):
        lw = (lower_bounds[l], w_in[l], conv_w[l], a_log[l], dt_bias[l], hgrn_norm_w[l],
              gdn_norm_w[l], w_oa[l], w_ob[l], w_out[l])
        Sa0 = jnp.zeros((B, H_A, DK_A, DV_A), f32)
        Sb0 = jnp.zeros((B, H_B, DK_B, DV_B), f32)
        cb0 = jnp.zeros((B, CONV_W - 1, D_CONV), xp.dtype)
        mix_p, Sa_p, Sb_p, cb_p = _token_mixer(_rmsnorm(xp, norm_mix[l]), Sa0, Sb0, cb0, *lw, chunked=True)
        xp = xp + mix_p
        xp = xp + _moe(_rmsnorm(xp, norm_ffn[l]), w_router[l], b_router[l], w_gu[l], b_gu[l], w_down[l], b_down[l])
        mix_s, Sa_s, Sb_s, cb_s = _token_mixer(_rmsnorm(xs, norm_mix[l]), state_hgrn[l], state_gdn[l],
                                               state_conv[l], *lw, chunked=False)
        xs = xs + mix_s
        xs = xs + _moe(_rmsnorm(xs, norm_ffn[l]), w_router[l], b_router[l], w_gu[l], b_gu[l], w_down[l], b_down[l])
        hp_list.append(Sa_p)
        gp_list.append(Sb_p)
        cp_list.append(cb_p)
        hs_list.append(Sa_s)
        gs_list.append(Sb_s)
        cs_list.append(cb_s)
    y_prompt = _rmsnorm(xp[:, N_META:], norm_final)
    y_sample = _rmsnorm(xs, norm_final)
    return (y_prompt, y_sample, jnp.stack(hp_list), jnp.stack(gp_list), jnp.stack(cp_list),
            jnp.stack(hs_list), jnp.stack(gs_list), jnp.stack(cs_list))


_drawn_inputs = setup_inputs


def setup_inputs(seed=0):
    import zlib

    import numpy as np

    out = dict(_drawn_inputs(seed))
    spreads = {}
    factors = {'hgrn_norm_w': 9.909,
     'b_gu': 8.0,
     'b_down': 45.862,
     'norm_final': 186.2,
     'gdn_norm_w': 10.508,
     'norm_ffn': 2.919,
     'b_router': 3.189}
    for name, (base, spread) in spreads.items():
        noise = np.random.default_rng([zlib.crc32(name.encode()), seed]).standard_normal(out[name].shape)
        drawn = base * np.exp(spread * noise) if base else spread * noise
        out[name] = jnp.asarray(drawn.astype(out[name].dtype))
    for name, factor in factors.items():
        out[name] = (out[name] * factor).astype(out[name].dtype)
    return out
```

```python
import concourse.bass as bass
from concourse import mybir
from contextlib import ExitStack

F32 = mybir.dt.float32
BF16 = mybir.dt.bfloat16
I32 = mybir.dt.int32
U32 = mybir.dt.uint32
ALU = mybir.AluOpType
ACT = mybir.ActivationFunctionType
AX = mybir.AxisListType

RMS_EPS = 1e-6
L2_EPS = 1e-6
SWIGLU_LIMIT = 7.0
SWIGLU_ALPHA = 1.702
TOP_K = 4


def hybrid_decoder_step(nc, x_prompt, x_sample, state_hgrn, state_gdn, state_conv, meta_tokens, lb_param,
                        norm_mix, w_in, conv_w, a_log, dt_bias, hgrn_norm_w, gdn_norm_w, w_oa, w_ob, w_out,
                        norm_ffn, w_router, b_router, w_gu, b_gu, w_down, b_down, norm_final,
                        y_prompt, y_sample, hgrn_prompt, gdn_prompt, conv_prompt,
                        hgrn_sample, gdn_sample, conv_sample):
    _, SEQ, D = x_prompt.shape
    NS = x_sample.shape[0]
    NM = meta_tokens.shape[0]
    _, _, H, DK, DV = state_hgrn.shape
    CW = conv_w.shape[1]
    DC = state_conv.shape[3]
    NE = w_gu.shape[1]
    KT = D // 128
    FC = DC // 128
    LEAD = 16
    T = LEAD + NM + SEQ
    TP = 96
    NI = T // TP
    C = 32
    NCC = TP // C
    HT = H * T
    CAP = 64
    NBX = NE + (T * TOP_K) // CAP
    NBT = NBX + 1
    SCALE = float(DK) ** -0.5
    HF = D // 2
    AB0 = 4 * H * DK + DC
    WCH = 512
    NCHUNK = (w_in.shape[2] - 2 * H) // WCH
    NRING = 3
    Q_, F_, I_, G_, QB_, KB_, VB_, Z_, GA_, GB_ = 0, 4, 8, 12, 16, 20, 24, 28, 32, 40
    NFT = 48
    SMALL = 880
    DOWN0 = 8

    ctx = ExitStack()
    with ctx:
        def sb(name, shape, dt=F32):
            return ctx.enter_context(nc.sbuf_tensor(name, shape, dt))

        def sem(name):
            return ctx.enter_context(nc.semaphore(name))

        def dram(name, shape, dt=F32):
            return nc.dram_tensor(name, shape, dt, kind="Internal").ap()

        ring = sb("ring", [128, 12, 2048])
        proj = sb("proj", [128, NFT, T])
        states = sb("states", [128, NS * H, DV])
        x_tok = sb("x_tok", [TP, NI, D])
        feat = sb("feat", [128, KT, T])
        wide = sb("wide", [128, 3, HT])
        ident = sb("ident", [128, 128])
        ones = sb("ones", [128, 128])
        tri = sb("tri", [TP, NCC, C])
        same = sb("same", [TP, NCC, C])
        causal = sb("causal", [TP, C])
        strict = sb("strict", [TP, C])
        keep = sb("keep", [128, T], BF16)
        w_ab = sb("w_ab", [128, KT, 2 * H])
        w_rt = sb("w_rt", [128, KT, NE])
        sm = sb("sm", [128, SMALL])
        epsb = sb("epsb", [128, 1])

        ringf = ring[:].rearrange("p s n -> p (s n)")
        win_buf = [ringf[:, 4096 * j:4096 * (j + 1)].rearrange("p (k n) -> p k n", k=KT) for j in range(NRING)]
        woa_sb = ringf[:, 0:4096].rearrange("p (k n) -> p k n", k=H)
        wob_sb = ringf[:, 4096:8192].rearrange("p (k n) -> p k n", k=H)
        wout_lo = ringf[:, 8192:12288].rearrange("p (k n) -> p k n", k=H)
        statesf = states[:].rearrange("p s n -> p (s n)")
        wout_hi = statesf.rearrange("p (k n) -> p k n", k=H)
        work = ringf[:, 12288:24576]

        def wk(at, n, parts=128):
            return work[0:parts, at:at + n]

        def tokmaj(at):
            return wk(at, 1536, TP).rearrange("p (i h n) -> p i h n", i=NI, h=H)

        kdA, vtA, kbe, kdB, vb = (tokmaj(1536 * j) for j in range(5))

        def blocks(at):
            return wk(at, 384, TP).rearrange("p (i h t) -> p i h t", i=NI, h=H)

        PT, LT, AT, MT, XT = (blocks(7680 + 384 * j) for j in range(5))
        NP = NI * NCC * H
        pairM = wk(9600, C * C, NP).rearrange("p (s t) -> p s t", s=C)
        pairX = wk(10624, C * C, NP).rearrange("p (s t) -> p s t", s=C)
        pairW = wk(11648, 256, NP)
        v_new = wk(9600, H * DV, TP)
        prm_rows = wk(4608, 128, 66)
        bufT = wk(11904, FC * NS * (CW - 1)).rearrange("p (f b j) -> p f b j", f=FC, b=NS)
        xh = wk(0, NI * D, TP).rearrange("p (i d) -> p i d", i=NI)
        buf_rows = wk(3072, DC, NS * (CW - 1))
        featf = feat[:].rearrange("p k t -> p (k t)")
        v_row = featf[0:NS, 0:H * DV]
        conv_new = featf[0:NS + 3, 768:768 + DC]
        xnT = proj[:, GA_:GA_ + KT, :]
        projf = proj[:].rearrange("p f t -> p (f t)")
        b_f32 = projf[0:3 * NE, 0:3 * D]
        hid_g, hid_u, hid_s, hid = (projf[:, 3072 + 512 * j:3584 + 512 * j] for j in range(4))
        hidT = projf[:, 5120:5632].rearrange("p (c t) -> p c t", c=4)
        y_out = projf[:, 5632:6144]
        xg = projf[0:CAP, 6144:7168]
        xgT = projf[:, 7168:7680].rearrange("p (k t) -> p k t", k=KT)
        sel_gu = projf[0:3 * NE, 7680:7680 + CAP // 2].bitcast(BF16)
        sel_dn = projf[0:3 * NE, 7712:7712 + CAP // 2].bitcast(BF16)
        nfin_b = projf[0:TP, 7744:7744 + D]
        nffn_b = projf[0:TP, 11520:11520 + D]
        x2h = statesf[0:TP, 0:NI * D].rearrange("p (i d) -> p i d", i=NI)
        spA, spB = (wide[:, 2, 512 * j:512 * j + 512].rearrange("p (h v) -> p h v", h=H) for j in range(2))
        cv = [wk(3072 + 1536 * g, HT) for g in range(3)]
        y_rows = [[ringf[0:TP, D * (TOP_K * i + j):D * (TOP_K * i + j) + D] for j in range(TOP_K)] for i in range(NI)]
        W0, W1, W2 = (wide[:, j, :] for j in range(3))
        wideh = lambda j: wide[:, j, :].rearrange("p (h t) -> p h t", h=H)

        at = [0]

        def small(n, dt=F32, parts=128):
            a = sm[0:parts, at[0]:at[0] + n]
            at[0] += n
            assert at[0] <= SMALL
            return a.bitcast(dt) if dt != F32 else a

        prmT = small(66)
        lbt, omlb = small(H), small(H)
        smq, smk, smf, gmq, gmk = (small(H * NS).rearrange("p (h b) -> p h b", h=H) for _ in range(5))
        sbeg, sbbeta, sdelta = (small(H * NS).rearrange("p (h b) -> p h b", h=H) for _ in range(3))
        decA = small(H * NI * NCC).rearrange("p (h c) -> p h c", h=H)
        ab = small(24, parts=TP).rearrange("p (i h) -> p i h", i=NI)
        gt, bt, Gt, Gl, bG, eGl, btm = (small(12, parts=TP).rearrange("p (i h) -> p i h", i=NI) for _ in range(7))
        alb, dtb = small(H, parts=TP), small(H, parts=TP)
        ss, rstd = small(NI, parts=TP), small(NI, parts=TP)
        conv_pack = small(FC * (NS + 3)).rearrange("p (f c) -> p f c", f=FC)
        smx, smy = (small(FC * NS).rearrange("p (f b) -> p f b", f=FC) for _ in range(2))
        soA, soB = (small(H * NS).rearrange("p (h b) -> p h b", h=H) for _ in range(2))
        nbi = small(1, I32, 1)
        tkc = small(1, I32, CAP)
        rt = [0]
        wr = wide[:].rearrange("p a n -> p (a n)")

        def rsmall(n, dt=F32, parts=TP):
            a = wr[0:parts, rt[0]:rt[0] + n]
            rt[0] += n
            assert rt[0] <= 3 * HT
            return a.bitcast(dt) if dt != F32 else a

        br_b = rsmall(NE)
        lg = rsmall(NI * NE).rearrange("p (i e) -> p i e", i=NI)
        selm = rsmall(NI * NE).rearrange("p (i e) -> p i e", i=NI)
        slot = rsmall(NI * NE).rearrange("p (i e) -> p i e", i=NI)
        rtmp = rsmall(NI * NE).rearrange("p (i e) -> p i e", i=NI)
        oneh = rsmall(NI * TOP_K * NE).rearrange("p (i j e) -> p i j e", i=NI, j=TOP_K)
        m8 = rsmall(NI * 8).rearrange("p (i e) -> p i e", i=NI)
        i8 = rsmall(NI * 8, U32).rearrange("p (i e) -> p i e", i=NI)
        i8f = rsmall(NI * 8).rearrange("p (i e) -> p i e", i=NI)
        gate = rsmall(NI * TOP_K).rearrange("p (i e) -> p i e", i=NI)
        gsum = rsmall(NI)
        slotf = rsmall(NI * TOP_K).rearrange("p (i e) -> p i e", i=NI)
        sloti = rsmall(NI * TOP_K, I32).rearrange("p (i e) -> p i e", i=NI)
        slotw = rsmall(NI * TOP_K, I32).rearrange("p (i e) -> p i e", i=NI)
        iota_e = rsmall(NE)
        expb = rsmall(NE)
        cnt = rsmall(NE)
        extra = rsmall(NE)
        offs = rsmall(NE)
        offx = rsmall(NE)
        tokid = rsmall(NI)
        triT = rsmall(TP)
        iota_b = rsmall(NBT, parts=NE)
        eh = rsmall(NBT, parts=NE)
        offc = rsmall(2, parts=NE)
        ehx = rsmall(NBT, parts=NE)
        eh3 = rsmall(NBT, parts=3 * NE)
        b3 = rsmall(3 * D // 2, parts=3 * NE).bitcast(BF16)
        blke = rsmall(NBT, I32, 1)
        blkf = rsmall(NBT, parts=1)
        nblk = rsmall(1, parts=1)
        iota_p = rsmall(1, parts=NE)
        tokT = rsmall(NBT, I32, CAP)
        tok_rows = rsmall(CAP, parts=NBT)
        hole, dump = rsmall(1), rsmall(TOP_K)
        extc = rsmall(2, parts=NE)
        sel4 = rsmall(NE)

        ps = ctx.enter_context(nc.psum_tensor("ps", [128, 8, 512], F32))
        psf = ps[:].rearrange("p b n -> p (b n)")
        bank = lambda j: ps[:, j, :]

        xn_dram = dram("xn_dram", [T, D])
        y_dram = dram("y_dram", [NBT * CAP, D])
        tok_dram = dram("tok_dram", [NBT * CAP, 1])
        pair_dram = dram("pair_dram", [NP, C, C])
        inv_dram = dram("inv_dram", [NP, C, C])

        sg = {name: sem(name) for name in """
            x_in0 x_in1 x_in2 prm_in buf_in ab_in par_in 
            win_in0 win_in1 win_in2
            consts lead_zero  tok_zeroed y_zeroed pairX_one
            x_summed x_normed x_turned feat_ready   lb_exp  
              ptile_done bank_free
            a_sig  a_ln  a_exp a_expb  a_kexp  vA_turned vA_taken scA_ops  
             kA_turned kA_taken
            conv_out conv_sig conv_done sq_ready l2_done l2_root b_normed  
             g_exp  beta_sig     lt_exp  G_diffs G_exps
             pair_stored pair_in  inv_stored XT_in
            kB_turned kB_taken vB_turned vB_taken  wT_taken 
            kvA_done vnew_done vnew_taken stepB_done o_taken state_upd
            stA_in stB_in stA_decayed stB_decayed stA_spread stA_new     stB_row
            stB_spread stB_new  oA_sample oB_sample stA_stored stB_stored spread_used
              conv_rows conv_stored prompt_stored
            n_sq n_sum n_root n_sig ya_ready gates_sig
            woa_in wob_in wout_in wout2_in  proj_out_used merged_ready oab_done mix_done x2_ready
            x2_summed x2_normed x2_turned xnT_ready  route_in nffn_in bias_in nfin_in
            route_consts top_exp        
            tok_scattered tok_back   xn_stored
            gu_used down_used wait_passed idx_ready xg_in xg_turned xg_ready sel_gu_ready sel_dn_ready b3_ready
            gate_clipped up_clipped sig_ready gu_mult hid_ready hid_turned hidT_ready y_ready y_stored
            yg_in0 yg_in1 yg_in2 yg_summed f_summed f_ready out_stored
             act_step pool_step dve_step
        """.split()}
        mark = {}
        for owner, names in (("vector_mark", """
                prm_ready lb_diff ab_taken g_pre g_ready conv_packed a_fg a_diff a_kdiff kA_ready PT_ready G_taken lt_diff MT_ready qdec_ready inv_ready stB_delta sel_done ext_ready slot_ready eh_ready nb_ready tokT_ready
                """), ("tensor_mark", """
                prm_turned ab_done cum_done scA_done conv_turned bcast_done scB_done stA_read wT_done stB_kS stB_turned stB_read logits_done cnt_done off_done blk_done tok_turned
                """)):
            shared = sem(owner)
            mark.update({name: (shared, n + 1) for n, name in enumerate(names.split())})
        w_arrived = [sem(f"w_arrived{j}") for j in range(12)]

        class Steps:

            def __init__(self, eng, name):
                self.eng, self.own, self.count = eng, sg[name], 0

            def __call__(self, ins):
                self.count += 1
                ins.then_inc(self.own, 1)
                self.eng.wait_ge(self.own, self.count)

            def tell(self, ins, name, n=1):
                own, count = mark[name] if name in mark else (sg[name], n)
                ins.then_inc(own, 1)
                self.eng.wait_ge(own, count)

        block = ctx.enter_context(nc.Block())

        @block.sync
        def _(sp):
            sp.dma_start(prm_rows[0:KT, :], norm_mix.rearrange("l (k p) -> (l k) p", p=128)).then_inc(sg["prm_in"], 16)
            sp.dma_start(prm_rows[8:16, :], lb_param.rearrange("r (h p) -> (r h) p", p=128)).then_inc(sg["prm_in"], 16)
            sp.dma_start(prm_rows[16:64, :], conv_w.rearrange("l j (f p) -> (l j f) p", p=128)).then_inc(sg["prm_in"], 16)
            sp.dma_start(prm_rows[64:65, :], hgrn_norm_w).then_inc(sg["prm_in"], 16)
            sp.dma_start(prm_rows[65:66, :], gdn_norm_w).then_inc(sg["prm_in"], 16)
            sp.dma_start(x_tok[:, 1, :], x_prompt[0, 64:160, :]).then_inc(sg["x_in1"], 16)
            sp.dma_start(x_tok[:, 2, :], x_prompt[0, 160:256, :]).then_inc(sg["x_in2"], 16)
            sp.wait_ge(sg["lead_zero"], 1)
            sp.dma_start(x_tok[0:NS, 0, :], x_sample[:, 0, :]).then_inc(sg["x_in0"], 16)
            sp.dma_start(x_tok[LEAD:LEAD + NM, 0, :], meta_tokens).then_inc(sg["x_in0"], 16)
            sp.dma_start(x_tok[LEAD + NM:TP, 0, :], x_prompt[0, 0:64, :]).then_inc(sg["x_in0"], 16)
            sp.dma_start(buf_rows, state_conv[0].rearrange("b j d -> (b j) d")).then_inc(sg["buf_in"], 16)
            sp.dma_start(w_ab[:], w_in[0, :, AB0:AB0 + 2 * H].rearrange("(k p) n -> p k n", p=128)).then_inc(sg["ab_in"], 16)
            for c in range(NCHUNK):
                col = WCH * c + (2 * H if WCH * c >= AB0 else 0)
                if c >= NRING:
                    sp.wait_ge(sg["ptile_done"], 4 * (c - NRING + 1))
                sp.dma_start(win_buf[c % NRING], w_in[0, :, col:col + WCH].rearrange("(k p) n -> p k n", p=128)) \
                    .then_inc(sg[f"win_in{c % NRING}"], 16)
            sp.wait_ge(sg["ptile_done"], NFT)
            sp.dma_start(woa_sb, w_oa[0].rearrange("(k p) n -> p k n", p=128)).then_inc(sg["woa_in"], 16)
            sp.dma_start(wob_sb, w_ob[0].rearrange("(k p) n -> p k n", p=128)).then_inc(sg["wob_in"], 16)
            sp.dma_start(wout_lo, w_out[0, 0:512, :].rearrange("(k p) n -> p k n", p=128)).then_inc(sg["wout_in"], 16)
            sp.wait_ge(*mark["MT_ready"])
            for c in range(NCC):
                sp.dma_start(pair_dram[12 * c:12 * c + 12].rearrange("q s t -> s q t"),
                             MT[C * c:C * c + C].rearrange("s i h t -> s (i h) t")).then_inc(sg["pair_stored"], 16)
            sp.wait_ge(sg["pair_stored"], 16 * NCC)
            sp.dma_start(pairM, pair_dram).then_inc(sg["pair_in"], 16)
            sp.wait_ge(*mark["inv_ready"])
            sp.dma_start(inv_dram, pairX).then_inc(sg["inv_stored"], 16)
            sp.wait_ge(sg["inv_stored"], 16)
            for c in range(NCC):
                sp.dma_start(XT[C * c:C * c + C].rearrange("s i h t -> s (i h) t"),
                             inv_dram[12 * c:12 * c + 12].rearrange("q s t -> s q t")).then_inc(sg["XT_in"], 16)
            sp.wait_ge(sg["stB_stored"], 16)
            sp.wait_ge(*mark["stB_read"])
            sp.dma_start(wout_hi, w_out[0, 512:1024, :].rearrange("(k p) n -> p k n", p=128)).then_inc(sg["wout2_in"], 16)
            sp.wait_ge(sg["state_upd"], NI * NCC)
            sp.dma_start(hgrn_prompt[0, 0].rearrange("h k v -> k h v"), spA).then_inc(sg["prompt_stored"], 16)
            sp.dma_start(gdn_prompt[0, 0].rearrange("h k v -> k h v"), spB).then_inc(sg["prompt_stored"], 16)
            sp.wait_ge(sg["oab_done"], KT)

            def gu_load(e, k):
                src = w_gu[0, e, 128 * k:128 * k + 128, :] if isinstance(e, int) else \
                    w_gu[0][bass.ds(e, 1), 128 * k:128 * k + 128, :].rearrange("a p n -> (a p) n")
                sp.dma_start(ring[:, k, :], src).then_inc(w_arrived[k], 16)

            def down_load(e, k):
                src = w_down[0, e, 256 * k:256 * k + 256, :] if isinstance(e, int) else \
                    w_down[0][bass.ds(e, 1), 256 * k:256 * k + 256, :].rearrange("a p n -> (a p) n")
                sp.dma_start(ring[:, KT + k, :].rearrange("p (j n) -> p j n", j=2),
                             src.rearrange("(j p) n -> p j n", p=128)).then_inc(w_arrived[KT + k], 16)

            def gu_loads(b, e):
                for k in range(KT):
                    sp.wait_ge(sg["gu_used"], 8 * b - 8 + k + 1)
                    gu_load(e, k)

            def down_loads(b, e):
                for k in range(4):
                    sp.wait_ge(sg["down_used"], DOWN0 + 4 * b - 4 + k + 1)
                    down_load(e, k)

            for k in range(4):
                gu_load(0, k)
            sp.wait_ge(sg["ya_ready"], 2)
            sp.wait_ge(sg["prompt_stored"], 32)
            for k in (6, 7):
                gu_load(0, k)
            sp.wait_ge(sg["mix_done"], 2 * NI)
            for k in (4, 5):
                gu_load(0, k)
            gu_loads(1, 1)
            for k in range(4):
                down_load(0, k)
            with sp.Fori(2, NE) as b:
                gu_loads(b, b)
                down_loads(b - 1, b - 1)
            sp.wait_ge(*mark["nb_ready"])
            nb = sp.value_load(nbi[0:1, 0:1], min_val=NE, max_val=NBX)
            with sp.If(nb > NE):
                with sp.Fori(NE, nb) as b:
                    gu_loads(b, sp.value_load(blke[0:1, bass.ds(b, 1)], min_val=0, max_val=NE - 1))
                    down_loads(b - 1, sp.value_load(blke[0:1, bass.ds(b - 1, 1)], min_val=0, max_val=NE - 1))
            down_loads(nb - 1, sp.value_load(blke[0:1, bass.ds(nb - 1, 1)], min_val=0, max_val=NE - 1))
            sp.wait_ge(sg["prompt_stored"], 32)

        @block.gpsimd
        def _(pool):
            L = Steps(pool, "pool_step")
            gp = nc.gpsimd
            gp.memset(x_tok[0:32, 0, :], 0.0).then_inc(sg["lead_zero"], 1)

            def masked(out, pattern, base, mult, op=ALU.is_ge, fill=0.0):
                L(gp.affine_select(out=out, in_=out, compare_op=op, fill=fill, base=base, pattern=pattern,
                                   channel_multiplier=mult))

            L(gp.memset(ident[:], 0.0))
            masked(ident[:], [[-1, 128]], 0, 1, ALU.not_equal, 1.0)
            L(gp.memset(epsb[:], RMS_EPS))
            L(gp.memset(ones[:], 1.0))
            L(gp.memset(tri[:], 1.0))
            masked(tri[:], [[C, NCC], [1, C]], 0, -1)
            masked(tri[:], [[-C, NCC], [0, C]], 0, 1)
            L(gp.memset(same[:], 1.0))
            masked(same[:], [[-C, NCC], [0, C]], 0, 1)
            masked(same[:], [[C, NCC], [0, C]], C - 1, -1)
            for m, base in ((causal, 0), (strict, -1)):
                L(gp.memset(m[:], 1.0))
                for c in range(NCC):
                    masked(m[C * c:C * c + C], [[1, C]], base, -1)
            L(gp.memset(keep[:], 1.0))
            L(gp.memset(keep[:].rearrange("p (c t) -> p c t", t=C)[:, :, 0:1], 0.0))
            L(gp.memset(tok_rows, 0.0))
            gp.dma_start(tok_dram.rearrange("(b r) o -> b (r o)", r=CAP), tok_rows).then_inc(sg["tok_zeroed"], 16)
            pool.wait_ge(sg["tok_zeroed"], 16)
            gp.sem_inc(sg["consts"], 1)
            L(gp.memset(wide[0:CAP, 0, 0:D], 0.0))
            gp.dma_start(y_dram[NE * CAP:NBT * CAP, :].rearrange("(b r) d -> r b d", r=CAP),
                         wide[0:CAP, 0:1, 0:D].to_broadcast([CAP, NBT - NE, D])).then_inc(sg["y_zeroed"], 16)
            pool.wait_ge(sg["x_turned"], NI)
            L(gp.memset(pairX, 0.0))
            gp.affine_select(out=pairX, in_=pairX, compare_op=ALU.not_equal, fill=1.0, base=0,
                             pattern=[[1, C], [-1, C]], channel_multiplier=0).then_inc(sg["pairX_one"], 1)
            pool.wait_ge(sg["stA_in"], 16)
            pool.wait_ge(*mark["a_fg"])
            st4 = states[:].rearrange("p (b h) v -> p b h v", h=H)
            for b in range(NS):
                last = gp.tensor_tensor(st4[:, b], st4[:, b], smf[:, :, b:b + 1].to_broadcast([128, H, DV]), ALU.mult)
                L(last)
            gp.sem_inc(sg["stA_decayed"], 1)
            pool.wait_ge(sg["stB_in"], 16)
            pool.wait_ge(sg["G_exps"], 2)
            for b in range(NS):
                L(gp.tensor_tensor(st4[:, b], st4[:, b], sbeg[:, :, b:b + 1].to_broadcast([128, H, DV]), ALU.mult))
            gp.sem_inc(sg["stB_decayed"], 1)
            pool.wait_ge(sg["prompt_stored"], 32)
            pool.wait_ge(sg["oab_done"], KT)
            pool.wait_ge(sg["merged_ready"], KT)
            iot = lambda out, pattern, base, mult: L(gp.iota(out, pattern=pattern, base=base, channel_multiplier=mult,
                                                             allow_small_or_imprecise_dtypes=True))
            iot(iota_e, [[1, NE]], 0, 0)
            iot(iota_b, [[1, NBT]], 0, 0)
            iot(iota_p, [[0, 1]], 0, 1)
            iot(tokid, [[TP, NI]], 0, 1)
            iot(dump, [[LEAD - NS, TOP_K]], NBX * CAP, 1)
            L(gp.memset(triT, 1.0))
            masked(triT, [[1, TP]], -1, -1)
            L(gp.memset(hole, 1.0))
            masked(hole, [[0, 1]], -NS, 1)
            masked(hole, [[0, 1]], LEAD - 1, -1)
            gp.sem_inc(sg["route_consts"], 1)
            pool.wait_ge(sg["bias_in"], 96)
            for p in range(3):
                r = slice(NE * p, NE * p + NE)
                for q in range(p + 1):
                    L(gp.tensor_copy(b3[r, :], b_f32[r, :]))
                    if q < p:
                        L(gp.tensor_tensor(b_f32[r, :], b_f32[r, :], b3[r, :], ALU.subtract))
            gp.sem_inc(sg["b3_ready"], 1)
            pool.wait_ge(*mark["slot_ready"])
            for i in range(NI):
                for j in range(TOP_K):
                    gp.indirect_dma_start(tok_dram, bass.IndirectOffsetOnAxis(ap=slotw[:, i, j:j + 1], axis=0),
                                          tokid[:, i:i + 1], None).then_inc(sg["tok_scattered"], 16)
            pool.wait_ge(sg["tok_scattered"], 16 * NI * TOP_K)
            gp.dma_start(tok_rows, tok_dram.rearrange("(b r) o -> b (r o)", r=CAP)).then_inc(sg["tok_back"], 16)
            pool.wait_ge(*mark["nb_ready"])
            nb = pool.value_load(nbi[0:1, 0:1], min_val=NE, max_val=NBX)
            pool.wait_ge(*mark["tokT_ready"])
            pool.wait_ge(sg["xn_stored"], 16 * NI)

            def gather():
                gp.indirect_dma_start(xg, None, xn_dram, bass.IndirectOffsetOnAxis(ap=tkc, axis=0)) \
                    .then_inc(sg["xg_in"], 16)

            gp.tensor_copy(tkc, tokT[:, 0:1]).then_inc(sg["idx_ready"], 1)
            pool.wait_ge(sg["idx_ready"], 1)
            gather()
            with pool.Fori(1, nb + 1) as b:
                pool.wait_ge(sg["xg_in"], 16 * b)
                pool.wait_ge(sg["xg_turned"], b)
                pool.wait_ge(*mark["tokT_ready"])
                gp.tensor_copy(tkc, tokT[:, bass.ds(b, 1)]).then_inc(sg["idx_ready"], 1)
                pool.wait_ge(sg["idx_ready"], b + 1)
                pool.sem_inc(sg["wait_passed"], 1)
                gather()
            pool.wait_ge(sg["down_used"], DOWN0 + 4 * nb)
            pool.wait_ge(sg["y_stored"], 32 * nb + 32)
            pool.wait_ge(sg["y_zeroed"], 16)
            pool.sem_inc(sg["wait_passed"], 1)
            for i in range(NI):
                for j in range(TOP_K):
                    gp.indirect_dma_start(y_rows[i][j], None, y_dram,
                                          bass.IndirectOffsetOnAxis(ap=sloti[:, i, j:j + 1], axis=0)) \
                        .then_inc(sg[f"yg_in{i}"], 16)

        @block.tensor
        def _(pe):
            mm = nc.tensor.matmul
            tr = nc.tensor.transpose
            pe.wait_ge(sg["consts"], 1)
            pe.wait_ge(sg["prm_in"], 80)
            pe.wait_ge(sg["buf_in"], 16)
            tr(bank(0)[:, 0:66], prm_rows[0:66, :], ident[0:66, 0:66])
            for f in range(FC):
                last = tr(bank(1)[:, 24 * f:24 * f + 24], buf_rows[:, 128 * f:128 * f + 128], ident[0:24, 0:24])
            last.then_inc(mark["prm_turned"][0], 1)
            for i in range(NI):
                pe.wait_ge(sg["x_normed"], i + 1)
                for k in range(KT):
                    last = tr(bank(2 + 2 * i + k // 4)[:, TP * (k % 4):TP * (k % 4) + TP], xh[:, i, 128 * k:128 * k + 128],
                              ident[0:TP, 0:TP])
                last.then_inc(sg["x_turned"], 1)
            pe.wait_ge(sg["feat_ready"], 2 * NI)
            pe.wait_ge(*mark["prm_ready"])
            pe.wait_ge(sg["ab_in"], 16)
            for i in range(NI):
                for k in range(KT):
                    last = mm(bank(0)[0:TP, 8 * i:8 * i + 8], feat[:, k, TP * i:TP * i + TP], w_ab[:, k, :],
                              start=k == 0, stop=k == KT - 1)
            last.then_inc(mark["ab_done"][0], 1)
            with pe.Fori(0, NCHUNK // NRING) as it:
                for j in range(NRING):
                    pe.wait_ge(sg[f"win_in{j}"], 16 * (it + 1))
                    for m in range(4):
                        pe.wait_ge(sg["bank_free"], 12 * it + (4 * j + m) + 1)
                        for k in range(KT):
                            last = mm(bank(4 + m)[:, 0:T], win_buf[j][:, k, 128 * m:128 * m + 128], feat[:, k, :],
                                      start=k == 0, stop=k == KT - 1)
                        last.then_inc(sg["ptile_done"], 1)
            pe.wait_ge(sg["bank_free"], 4 + NFT)

            for i in range(NI):
                for h in range(H):
                    last = tr(bank(4 + i)[0:TP, 128 * h:128 * h + 128], proj[:, I_ + h, TP * i:TP * i + TP], ident[:])
                last.then_inc(sg["vA_turned"], 1)
            pe.wait_ge(*mark["g_ready"])
            mm(bank(3)[0:TP, 0:12], tri[:].rearrange("p a b -> p (a b)"), gt.rearrange("p i h -> p (i h)"))
            mm(bank(3)[0:TP, 16:28], same[:].rearrange("p a b -> p (a b)"), gt.rearrange("p i h -> p (i h)")) \
                .then_inc(mark["cum_done"][0], 1)
            pe.wait_ge(sg["scA_ops"], 2)
            for i in range(NI):
                for c in range(NCC):
                    col = TP * i + C * c
                    for h in range(H):
                        last = mm(bank(7)[C * c:C * c + C, C * (H * i + h):C * (H * i + h) + C], proj[:, F_ + h, col:col + C],
                                  wideh(0)[:, h, col:col + C], start=True, stop=True)
            last.then_inc(mark["scA_done"][0], 1)
            pe.wait_ge(*mark["kA_ready"])
            pe.wait_ge(sg["vA_taken"], NI)
            for i in range(NI):
                for h in range(H):
                    last = tr(bank(4 + i)[0:TP, 128 * h:128 * h + 128], proj[:, Q_ + h, TP * i:TP * i + TP], ident[:])
                last.then_inc(sg["kA_turned"], 1)
            pe.wait_ge(*mark["ab_taken"])
            for g in range(2):
                pe.wait_ge(sg["sq_ready"], g + 1)
                if g:
                    pe.wait_ge(sg["l2_root"], 1)
                for n in range(0, HT, 512):
                    e = min(n + 512, HT)
                    last = mm(psf[:, n:e], ones[:], cv[g][:, n:e], start=True, stop=True)
                last.then_inc(sg["l2_done"], 1)
            pe.wait_ge(*mark["conv_packed"])
            pe.wait_ge(sg["l2_root"], 2)
            for f in range(FC):
                last = tr(bank(f // 4)[0:NS + 3, 128 * (f % 4):128 * (f % 4) + 128], conv_pack[:, f, :], ident[:])
            last.then_inc(mark["conv_turned"][0], 1)
            pe.wait_ge(sg["kA_taken"], NI)
            pe.wait_ge(*mark["PT_ready"])
            pe.wait_ge(sg["conv_rows"], 1)
            pe.wait_ge(*mark["G_taken"])
            for h in range(H):
                for i in range(NI):
                    mm(bank(4 + h)[:, TP * i:TP * i + TP], gt[:, i, h:h + 1].to_broadcast([TP, 128]),
                       tri[:].rearrange("p a b -> p (a b)"), start=True, stop=True)
                    mm(bank(h)[:, TP * i:TP * i + TP], bt[:, i, h:h + 1].to_broadcast([TP, 128]), ident[0:TP, 0:TP],
                       start=True, stop=True)
                last = mm(bank(4 + h)[:, T:T + NS], gt[:, 0, h:h + 1].to_broadcast([TP, 128]), ident[0:TP, 0:NS],
                          start=True, stop=True)
            last.then_inc(mark["bcast_done"][0], 1)
            pe.wait_ge(sg["G_diffs"], NCC)
            pe.wait_ge(sg["G_exps"], 2)
            pe.wait_ge(sg["b_normed"], 2)
            qk = proj[:, QB_:KB_ + H, :].rearrange("p (a h) t -> p h a t", a=2)
            for i in range(NI):
                for c in range(NCC):
                    col = TP * i + C * c
                    for h in range(H):
                        n = H * i + h
                        last = mm(bank(4 + n // 8)[C * c:C * c + C, 64 * (n % 8):64 * (n % 8) + 64],
                                  proj[:, KB_ + h, col:col + C], qk[:, h, :, col:col + C], start=True, stop=True)
            last.then_inc(mark["scB_done"][0], 1)
            pe.wait_ge(*mark["MT_ready"])
            tb = (6, 7, 3)
            for i in range(NI):
                for h in range(H):
                    last = tr(bank(tb[i])[0:TP, 128 * h:128 * h + 128], proj[:, KB_ + h, TP * i:TP * i + TP], ident[:])
                last.then_inc(sg["kB_turned"], 1)
            pe.wait_ge(sg["kB_taken"], NI)
            pe.wait_ge(sg["conv_done"], 3)
            for i in range(NI):
                for h in range(H):
                    last = tr(bank(tb[i])[0:TP, 128 * h:128 * h + 128], proj[:, VB_ + h, TP * i:TP * i + TP], ident[:])
                last.then_inc(sg["vB_turned"], 1)

            def spread(name, base):
                for b in range(NS):
                    if base + b >= 2:
                        pe.wait_ge(sg["spread_used"], base + b - 1)
                    mm(bank(b % 2)[:, :], ident[0:NS, b:b + 1].to_broadcast([NS, 128]), v_row, start=True, stop=True) \
                        .then_inc(sg[name], 1)

            pe.wait_ge(sg["vA_taken"], NI + 1)
            spread("stA_spread", 0)
            pe.wait_ge(sg["stA_new"], NS * H)
            for b in range(NS):
                for h in range(H):
                    last = mm(bank(2)[:, NS * h + b:NS * h + b + 1], states[:, H * b + h, :], smq[:, h, b:b + 1],
                              start=True, stop=True)
            last.then_inc(mark["stA_read"][0], 1)
            pe.wait_ge(sg["vB_taken"], NI)
            pe.wait_ge(sg["XT_in"], 16 * NCC)
            for h in range(H):
                for i in range(NI):
                    for c in range(NCC):
                        last = mm(bank(4 + c)[:, C * (NI * h + i):C * (NI * h + i) + C], kbe[C * c:C * c + C, i, h, :],
                                  XT[C * c:C * c + C, i, h, :], start=True, stop=True)
            last.then_inc(mark["wT_done"][0], 1)
            pe.wait_ge(sg["stB_decayed"], 1)
            pe.wait_ge(sg["oA_sample"], 1)
            for b in range(NS):
                for h in range(H):
                    last = mm(bank(2)[:, NS * h + b:NS * h + b + 1], states[:, H * b + h, :], gmk[:, h, b:b + 1],
                              start=True, stop=True)
            last.then_inc(mark["stB_kS"][0], 1)
            pe.wait_ge(*mark["stB_delta"])
            for h in range(H):
                last = tr(bank(3)[0:NS, 128 * h:128 * h + 128], sdelta[:, h, :], ident[:])
            last.then_inc(mark["stB_turned"][0], 1)
            pe.wait_ge(sg["stB_row"], 1)
            spread("stB_spread", NS)
            pe.wait_ge(sg["stB_new"], NS * H)
            for b in range(NS):
                for h in range(H):
                    last = mm(bank(2)[:, NS * h + b:NS * h + b + 1], states[:, H * b + h, :], gmq[:, h, b:b + 1],
                              start=True, stop=True)
            last.then_inc(mark["stB_read"][0], 1)

            pe.wait_ge(sg["wT_taken"], 1)
            pe.wait_ge(*mark["qdec_ready"])
            pe.wait_ge(sg["oB_sample"], 1)
            for n in range(NI * NCC):
                i, c = n // NCC, n % NCC
                col, rows = TP * i + C * c, slice(C * c, C * c + C)
                first = n == 0
                if n:
                    pe.wait_ge(sg["state_upd"], n)
                    pe.wait_ge(sg["o_taken"], n)
                for h in range(H):
                    last = mm(bank(4)[rows, 128 * h:128 * h + 128], XT[rows, i, h, :], vb[rows, i, h, :], start=True, stop=first)
                    if not first:
                        last = mm(bank(4)[rows, 128 * h:128 * h + 128], wideh(1)[:, h, col:col + C], spB[:, h, :],
                                  start=False, stop=True)
                last.then_inc(sg["vnew_done"], 1)
                for h in range(H):
                    mm(bank(0)[:, C * h:C * h + C], vtA[rows, i, h, :], PT[rows, i, h, :], start=True, stop=first)
                    if not first:
                        mm(bank(0)[:, C * h:C * h + C], spA[:, h, :], proj[:, I_ + h, col:col + C], start=False, stop=True)
                    last = mm(bank(2)[:, 128 * h:128 * h + 128], kdA[rows, i, h, :], vtA[rows, i, h, :], start=True, stop=True)
                last.then_inc(sg["kvA_done"], 1)
                pe.wait_ge(sg["vnew_taken"], n + 1)
                for h in range(H):
                    mm(bank(1)[:, C * h:C * h + C], v_new[rows, 128 * h:128 * h + 128], AT[rows, i, h, :], start=True, stop=first)
                    if not first:
                        mm(bank(1)[:, C * h:C * h + C], spB[:, h, :], proj[:, QB_ + h, col:col + C], start=False, stop=True)
                    last = mm(bank(5)[:, 128 * h:128 * h + 128], kdB[rows, i, h, :], v_new[rows, 128 * h:128 * h + 128],
                              start=True, stop=True)
                last.then_inc(sg["stepB_done"], 1)

            pe.wait_ge(sg["o_taken"], NI * NCC)
            for g in range(2):
                pe.wait_ge(sg["n_sq"], g + 1)
                if g:
                    pe.wait_ge(sg["n_root"], 1)
                for n in range(0, HT, 512):
                    e = min(n + 512, HT)
                    last = mm(psf[:, n:e], ones[:], wide[:, g, n:e], start=True, stop=True)
                last.then_inc(sg["n_sum"], 1)
            pe.wait_ge(sg["ya_ready"], 2)
            pe.wait_ge(sg["woa_in"], 16)
            pe.wait_ge(sg["wob_in"], 16)
            for m in range(KT):
                if m >= 4:
                    pe.wait_ge(sg["proj_out_used"], m - 3)
                for w, b, g in ((woa_sb, 2 * (m % 4), G_), (wob_sb, 2 * (m % 4) + 1, Z_)):
                    for k in range(H):
                        last = mm(bank(b)[:, 0:T], w[:, k, 128 * m:128 * m + 128], proj[:, g + k, :],
                                  start=k == 0, stop=k == H - 1)
                last.then_inc(sg["oab_done"], 1)
            pe.wait_ge(sg["merged_ready"], KT)
            pe.wait_ge(sg["wout_in"], 16)
            pe.wait_ge(sg["wout2_in"], 16)
            for i in range(NI):
                for j in range(2):
                    for k in range(KT):
                        w = wout_lo[:, k, :] if k < 4 else wout_hi[:, k - 4, :]
                        last = mm(bank(2 * i + j)[0:TP, :], feat[:, k, TP * i:TP * i + TP], w[:, 512 * j:512 * j + 512],
                                  start=k == 0, stop=k == KT - 1)
                    last.then_inc(sg["mix_done"], 1)
            for i in range(NI):
                pe.wait_ge(sg["x2_normed"], i + 1)
                if i == 1:
                    pe.wait_ge(sg["x2_ready"], 2 * NI)
                for k in range(KT):
                    last = tr(bank((6 + 2 * i) % 8 + k // 4)[:, TP * (k % 4):TP * (k % 4) + TP],
                              x2h[:, i, 128 * k:128 * k + 128], ident[0:TP, 0:TP])
                last.then_inc(sg["x2_turned"], 1)
            pe.wait_ge(sg["route_in"], 32)
            pe.wait_ge(sg["xnT_ready"], 2 * NI)
            for i in range(NI):
                for k in range(KT):
                    last = mm(bank(4)[0:TP, NE * i:NE * i + NE], xnT[:, k, TP * i:TP * i + TP], w_rt[:, k, :],
                              start=k == 0, stop=k == KT - 1)
            last.then_inc(mark["logits_done"][0], 1)
            pe.wait_ge(*mark["sel_done"])
            pe.wait_ge(sg["route_consts"], 1)
            for i in range(NI):
                mm(bank(5)[0:TP, NE * i:NE * i + NE], triT, selm[:, i, :], start=True, stop=i == 0)
                for p in range(i):
                    mm(bank(5)[0:TP, NE * i:NE * i + NE], ones[0:TP, 0:TP], selm[:, p, :], start=False, stop=p == i - 1)
            for i in range(NI):
                last = mm(bank(6)[0:NE, 0:1], selm[:, i, :], ones[0:TP, 0:1], start=i == 0, stop=i == NI - 1)
            last.then_inc(mark["cnt_done"][0], 1)
            pe.wait_ge(*mark["ext_ready"])
            mm(bank(6)[0:NE, 8:9], strict[0:NE, 0:NE], extc[:, 0:1], start=True, stop=True)
            mm(bank(6)[0:1, 16:17], extc[:, 0:1], ones[0:NE, 0:1], start=True, stop=True)
            mm(bank(6)[0:TP, 64:64 + NE], extc[:, 0:1].to_broadcast([NE, TP]), strict[0:NE, 0:NE], start=True, stop=True) \
                .then_inc(mark["off_done"][0], 1)
            pe.wait_ge(*mark["eh_ready"])
            mm(bank(6)[0:1, 128:128 + NBT], iota_p, eh, start=True, stop=True).then_inc(mark["blk_done"][0], 1)
            pe.wait_ge(sg["tok_back"], 16)
            tr(bank(7)[0:CAP, 0:NBT], tok_rows, ident[0:NBT, 0:NBT]).then_inc(mark["tok_turned"][0], 1)

            pe.wait_ge(*mark["nb_ready"])
            nb = pe.value_load(nbi[0:1, 0:1], min_val=NE, max_val=NBX)
            rows_T = bank(2).rearrange("p (k t) -> p k t", k=KT)
            hid_T = bank(3).rearrange("p (c t) -> p c t", c=4)
            pe.wait_ge(*mark["tokT_ready"])
            pe.wait_ge(sg["b3_ready"], 1)

            def turn_rows(b):
                pe.wait_ge(sg["xg_in"], 16 * (b + 1))
                pe.sem_inc(sg["wait_passed"], 1)
                for k in range(KT):
                    last = tr(rows_T[:, k, :], xg[:, 128 * k:128 * k + 128], ident[0:CAP, 0:CAP])
                last.then_inc(sg["xg_turned"], 1)

            def gate_up(b):
                pe.wait_ge(sg["xg_ready"], b + 1)
                pe.wait_ge(sg["sel_gu_ready"], b + 1)
                pe.wait_ge(sg["up_clipped"], b + 1)
                for j in range(4):
                    mm(bank(j // 2)[64 * (j % 2):64 * (j % 2) + 64, :], sel_gu, b3[:, 512 * j:512 * j + 512],
                       start=True, stop=False)
                for k in range(KT):
                    pe.wait_ge(w_arrived[k], 16 * (b + 1))
                    for j in range(4):
                        last = mm(bank(j // 2)[64 * (j % 2):64 * (j % 2) + 64, :], xgT[:, k, :],
                                  ring[:, k, 512 * j:512 * j + 512], start=False, stop=k == KT - 1)
                    last.then_inc(sg["gu_used"], 1)

            def down(b):
                pe.wait_ge(sg["hid_ready"], b + 1)
                pe.sem_inc(sg["wait_passed"], 1)
                for c in range(4):
                    last = tr(hid_T[:, c, :], hid[:, 128 * c:128 * c + 128], ident[:])
                last.then_inc(sg["hid_turned"], 1)
                pe.wait_ge(sg["sel_dn_ready"], b + 1)
                pe.wait_ge(sg["y_ready"], b + 1)
                for j in range(2):
                    mm(bank(4)[64 * j:64 * j + 64, :], sel_dn, b3[:, 2048 + 512 * j:2560 + 512 * j], start=True, stop=False)
                pe.wait_ge(sg["hidT_ready"], b + 1)
                for k in range(KT):
                    if k % 2 == 0:
                        pe.wait_ge(w_arrived[KT + k // 2], 16 * (b + 1))
                    for j in range(2):
                        n = (k % 2) * 1024 + 512 * j
                        last = mm(bank(4)[64 * j:64 * j + 64, :], hidT[:, k % 4, 64 * (k // 4):64 * (k // 4) + 64],
                                  ring[:, KT + k // 2, n:n + 512], start=False, stop=k == KT - 1)
                    if k % 2:
                        last.then_inc(sg["down_used"], 1)

            pe.sem_inc(sg["down_used"], DOWN0)
            turn_rows(0)
            gate_up(0)
            turn_rows(1)
            with pe.Fori(0, nb - 1) as b:
                gate_up(b + 1)
                turn_rows(b + 2)
                down(b)
            down(nb - 1)

        @block.scalar
        def _(act):
            L = Steps(act, "act_step")
            f = nc.scalar.activation
            act.dma_start(alb, a_log.to_broadcast([TP, H])).then_inc(sg["par_in"], 16)
            act.dma_start(dtb, dt_bias.to_broadcast([TP, H])).then_inc(sg["par_in"], 16)
            act.dma_start(states[:], state_hgrn[0].rearrange("b h k v -> k (b h) v")).then_inc(sg["stA_in"], 16)
            act.dma_start(w_rt[:], w_router[0].rearrange("(k p) n -> p k n", p=128)).then_inc(sg["route_in"], 16)
            act.dma_start(conv_sample[0, :, 0:CW - 2, :], state_conv[0, :, 1:CW - 1, :]).then_inc(sg["conv_stored"], 16)
            for i, n in enumerate((48, 16, 16)):
                act.wait_ge(sg[f"x_in{i}"], n)
                L(f(xh[:, i, :], x_tok[:, i, :], ACT.Square, accum_out=ss[:, i:i + 1]))
            act.wait_ge(sg["consts"], 1)
            L.tell(f(rstd, ss, ACT.Sqrt, scale=1.0 / D, bias=epsb[0:TP, 0:1]), "x_summed")
            act.wait_ge(sg["par_in"], 32)
            L(f(alb, alb, ACT.Exp))
            act.wait_ge(*mark["lb_diff"])
            L(f(lbt, lbt, ACT.Exp))
            L.tell(f(omlb, omlb, ACT.Exp), "lb_exp")
            act.wait_ge(*mark["g_pre"])
            L(f(Gl, Gl, ACT.Exp))
            L.tell(f(Gl, Gl, ACT.Ln, bias=1.0), "g_exp")
            L.tell(f(bt, ab[:, :, H:2 * H], ACT.Sigmoid), "beta_sig")
            with act.Fori(0, NFT // 4) as n:
                for m in range(4):
                    act.wait_ge(sg["ptile_done"], 4 * n + m + 1)
                    f(proj[:, bass.ds(4 * n + m, 1), :], bank(4 + m)[:, 0:T].rearrange("p (a t) -> p a t", a=1), ACT.Copy) \
                        .then_inc(sg["bank_free"], 1)
            act.wait_ge(sg["bank_free"], 4 + NFT)
            group = lambda g: proj[:, g:g + H, :]
            act.wait_ge(sg["y_zeroed"], 16)
            L.tell(f(wideh(0), group(Q_), ACT.Sigmoid), "a_sig", 1)
            L.tell(f(wideh(1), group(F_), ACT.Sigmoid), "a_sig", 2)
            L.tell(f(wideh(2), group(F_), ACT.Sigmoid, scale=-1.0), "a_sig", 3)
            heads = lambda b: bank(b)[0:TP, :].rearrange("p (h n) -> p h n", h=H)
            for i in range(NI):
                act.wait_ge(sg["vA_turned"], i + 1)
                L.tell(f(vtA[:, i], heads(4 + i), ACT.Copy), "vA_taken", i + 1)
            L.tell(f(v_row, bank(4)[0:NS, :], ACT.Copy), "vA_taken", NI + 1)
            act.wait_ge(*mark["a_fg"])
            L.tell(f(group(F_), wideh(1), ACT.Ln), "a_ln")
            act.wait_ge(*mark["a_diff"])
            L.tell(f(wideh(0), group(F_), ACT.Exp), "a_exp", 1)
            L.tell(f(group(F_), group(F_), ACT.Exp, scale=-1.0), "a_exp", 2)
            L.tell(f(group(I_), wideh(1), ACT.Exp), "a_expb")
            act.wait_ge(*mark["a_kdiff"])
            L.tell(f(group(Q_), group(Q_), ACT.Exp), "a_kexp")
            cvh = lambda g: cv[g].rearrange("p (h t) -> p h t", h=H)
            for g in range(3):
                act.wait_ge(sg["conv_out"], g + 1)
                L.tell(f(group(QB_ + H * g), cvh(g), ACT.Sigmoid), "conv_sig", g + 1)
            for i in range(NI):
                act.wait_ge(sg["kA_turned"], i + 1)
                L.tell(f(kdA[:, i], heads(4 + i), ACT.Copy), "kA_taken", i + 1)
            for g in range(2):
                act.wait_ge(sg["conv_done"], g + 1)
                L.tell(f(cvh(g), group(QB_ + H * g), ACT.Square), "sq_ready", g + 1)
                act.wait_ge(sg["l2_done"], g + 1)
                L.tell(f(cv[g], psf[:, 0:HT], ACT.Sqrt, bias=epsb[:, 0:1]), "l2_root", g + 1)
            act.wait_ge(*mark["conv_turned"])
            L.tell(f(conv_new, psf[0:NS + 3, 0:DC], ACT.Copy), "conv_rows")
            act.dma_start(conv_sample[0, :, CW - 2, :], conv_new[0:NS, :]).then_inc(sg["conv_stored"], 16)
            act.dma_start(conv_prompt[0, 0], conv_new[NS:NS + 3, :]).then_inc(sg["conv_stored"], 16)
            act.wait_ge(*mark["bcast_done"])
            L.tell(f(wideh(0), ps[:, 4:8, 0:T], ACT.Exp), "G_exps", 1)
            L.tell(f(sbeg, ps[:, 4:8, T:T + NS], ACT.Exp), "G_exps", 2)
            act.wait_ge(*mark["lt_diff"])
            L.tell(f(LT, LT, ACT.Exp), "lt_exp", 1)
            L.tell(f(bG, Gt, ACT.Exp), "lt_exp", 2)
            L.tell(f(eGl, eGl, ACT.Exp), "lt_exp", 3)
            act.wait_ge(*mark["stA_read"])
            L.tell(f(soA, bank(2)[:, 0:H * NS].rearrange("p (h b) -> p h b", h=H), ACT.Copy), "oA_sample")
            act.dma_start(hgrn_sample[0].rearrange("b h k v -> k (b h) v"), states[:]).then_inc(sg["stA_stored"], 16)
            act.wait_ge(sg["stA_stored"], 16)
            act.dma_start(states[:], state_gdn[0].rearrange("b h k v -> k (b h) v")).then_inc(sg["stB_in"], 16)
            act.wait_ge(*mark["wT_done"])
            L.tell(f(W1.rearrange("p (n c t) -> p c n t", c=NCC, t=C),
                     ps[:, 4:4 + NCC, 0:H * NI * C].rearrange("p c (n t) -> p c n t", t=C), ACT.Copy, scale=-1.0), "wT_taken")
            act.wait_ge(*mark["stB_turned"])
            L.tell(f(v_row, bank(3)[0:NS, :], ACT.Copy), "stB_row")
            act.wait_ge(*mark["stB_read"])
            L.tell(f(soB, bank(2)[:, 0:H * NS].rearrange("p (h b) -> p h b", h=H), ACT.Copy), "oB_sample")
            act.dma_start(gdn_sample[0].rearrange("b h k v -> k (b h) v"), states[:]).then_inc(sg["stB_stored"], 16)
            for n in range(NI * NCC):
                i, c = n // NCC, n % NCC
                col, rows = TP * i + C * c, slice(C * c, C * c + C)
                act.wait_ge(sg["vnew_done"], n + 1)
                L.tell(f(v_new[rows, :], bank(4)[rows, :], ACT.Copy), "vnew_taken", n + 1)
                act.wait_ge(sg["stepB_done"], n + 1)
                out = lambda b: bank(b)[:, 0:H * C].rearrange("p (h t) -> p h t", h=H)
                L(f(proj[:, Q_:Q_ + H, col:col + C], out(0), ACT.Copy))
                L.tell(f(proj[:, KB_:KB_ + H, col:col + C], out(1), ACT.Copy), "o_taken", n + 1)
            L(f(proj[:, Q_:Q_ + H, 0:NS], soA, ACT.Copy))
            L(f(proj[:, KB_:KB_ + H, 0:NS], soB, ACT.Copy))
            act.wait_ge(sg["state_upd"], NI * NCC)
            for g, grp in enumerate((Q_, KB_)):
                L.tell(f(wideh(g), group(grp), ACT.Square), "n_sq", g + 1)
            L.tell(f(group(F_), group(G_), ACT.Sigmoid), "n_sig", 1)
            L.tell(f(group(VB_), group(Z_), ACT.Sigmoid), "n_sig", 2)
            L.tell(f(proj[:, GA_:NFT, :], proj[:, GA_:NFT, :], ACT.Sigmoid), "gates_sig")
            for g in range(2):
                act.wait_ge(sg["n_sum"], g + 1)
                L.tell(f(wide[:, g, :], psf[:, 0:HT], ACT.Sqrt, scale=1.0 / DV, bias=epsb[:, 0:1]), "n_root", g + 1)
            act.wait_ge(sg["ya_ready"], 2)
            for p in range(3):
                act.dma_start(b_f32[NE * p:NE * p + NE, 0:2 * D], b_gu[0]).then_inc(sg["bias_in"], 16)
                act.dma_start(b_f32[NE * p:NE * p + NE, 2 * D:3 * D], b_down[0]).then_inc(sg["bias_in"], 16)
            act.dma_start(br_b, b_router.to_broadcast([TP, NE])).then_inc(sg["route_in"], 16)
            act.wait_ge(sg["merged_ready"], KT)
            act.dma_start(nffn_b, norm_ffn.to_broadcast([TP, D])).then_inc(sg["nffn_in"], 16)
            act.dma_start(nfin_b, norm_final.rearrange("(a d) -> a d", a=1).to_broadcast([TP, D])).then_inc(sg["nfin_in"], 16)
            act.wait_ge(sg["mix_done"], 2 * NI)
            for i in range(NI):
                act.wait_ge(sg["x2_ready"], 2 * i + 2)
                L(f(x2h[:, i, :], x_tok[:, i, :], ACT.Square, accum_out=ss[:, i:i + 1]))
                L.tell(f(rstd[:, i:i + 1], ss[:, i:i + 1], ACT.Sqrt, scale=1.0 / D, bias=epsb[0:TP, 0:1]), "x2_summed", i + 1)
            for i in range(NI):
                act.wait_ge(sg["x2_normed"], i + 1)
                act.dma_start(xn_dram[TP * i:TP * i + TP, :], x2h[:, i, :]).then_inc(sg["xn_stored"], 16)
                act.wait_ge(sg["x2_turned"], i + 1)
                for j in range(2):
                    src = bank((6 + 2 * i) % 8 + j)[:, 0:4 * TP].rearrange("p (k t) -> p k t", k=4)
                    L.tell(f(xnT[:, 4 * j:4 * j + 4, TP * i:TP * i + TP], src, ACT.Copy), "xnT_ready", 2 * i + j + 1)
            act.wait_ge(*mark["cnt_done"])
            L.tell(f(gate, gate, ACT.Exp), "top_exp")
            act.wait_ge(*mark["nb_ready"])
            nb = act.value_load(nbi[0:1, 0:1], min_val=NE, max_val=NBX)
            act.wait_ge(*mark["eh_ready"])
            act.sem_inc(sg["y_stored"], 32)
            act.sem_inc(sg["y_ready"], 1)

            def pick(out, b, name):
                f(out, eh3[:, bass.ds(b, 1)].to_broadcast([3 * NE, CAP]), ACT.Copy).then_inc(sg[name], 1)

            pick(sel_gu, 0, "sel_gu_ready")
            with act.Fori(0, nb) as b:
                pick(sel_dn, b, "sel_dn_ready")
                act.wait_ge(sg["gate_clipped"], b + 1)
                pick(sel_gu, b + 1, "sel_gu_ready")
                f(hid_s, hid_g, ACT.Sigmoid, scale=SWIGLU_ALPHA).then_inc(sg["sig_ready"], 1)
                act.wait_ge(sg["hid_turned"], b + 1)
                f(hidT, bank(3).rearrange("p (c t) -> p c t", c=4), ACT.Copy).then_inc(sg["hidT_ready"], 1)
                act.wait_ge(sg["down_used"], DOWN0 + 4 * b + 4)
                act.wait_ge(sg["y_stored"], 32 * (b + 1))
                f(y_out, bank(4), ACT.Copy).then_inc(sg["y_ready"], 1)
                act.wait_ge(sg["y_ready"], b + 2)
                for j in range(2):
                    act.dma_start(y_dram[bass.ds(b * CAP, CAP), HF * j:HF * j + HF], y_out[64 * j:64 * j + 64, :]) \
                        .then_inc(sg["y_stored"], 16)
            for i in range(NI):
                act.wait_ge(sg["yg_summed"], i + 1)
                L(f(x2h[:, i, :], x_tok[:, i, :], ACT.Square, accum_out=ss[:, i:i + 1]))
                L.tell(f(rstd[:, i:i + 1], ss[:, i:i + 1], ACT.Sqrt, scale=1.0 / D, bias=epsb[0:TP, 0:1]), "f_summed", i + 1)
            for i in range(NI):
                act.wait_ge(sg["f_ready"], i + 1)
                if i == 0:
                    act.dma_start(y_sample[:, 0, :], x_tok[0:NS, 0, :]).then_inc(sg["out_stored"], 16)
                    act.dma_start(y_prompt[0, 0:TP - 32, :], x_tok[32:TP, 0, :]).then_inc(sg["out_stored"], 16)
                else:
                    act.dma_start(y_prompt[0, TP * i - 32:TP * i + 64, :], x_tok[:, i, :]).then_inc(sg["out_stored"], 16)
            act.wait_ge(sg["out_stored"], 16 * (NI + 1))
            act.wait_ge(sg["conv_stored"], 48)

        @block.vector
        def _(dve):
            L = Steps(dve, "dve_step")
            v = nc.vector
            tt, ts, stt = v.tensor_tensor, v.tensor_scalar, v.scalar_tensor_tensor
            group = lambda g: proj[:, g:g + H, :]
            flat = lambda g: proj[:, g:g + H, :].rearrange("p h t -> p (h t)")
            last_dim = lambda a: a.rearrange("p i (h o) -> p i h o", o=1)
            dve.wait_ge(*mark["prm_turned"])
            L(v.tensor_copy(prmT, bank(0)[:, 0:66]))
            L.tell(v.tensor_copy(bufT.rearrange("p f b j -> p (f b j)"), bank(1)[:, 0:288]), "prm_ready")
            L(tt(lbt, prmT[:, 8:12], prmT[:, 12:16], ALU.max))
            L(tt(omlb, prmT[:, 12:16], lbt, ALU.subtract))
            L.tell(tt(lbt, prmT[:, 8:12], lbt, ALU.subtract), "lb_diff")
            dve.wait_ge(sg["x_summed"], 1)
            L(v.reciprocal(rstd, rstd))
            for i in range(NI):
                L.tell(ts(xh[:, i, :], x_tok[:, i, :], rstd[:, i:i + 1], None, ALU.mult), "x_normed", i + 1)
            for i in range(NI):
                dve.wait_ge(sg["x_turned"], i + 1)
                for j in range(2):
                    src = bank(2 + 2 * i + j)[:, 0:4 * TP].rearrange("p (k t) -> p k t", k=4)
                    w = prmT[:, 4 * j:4 * j + 4].rearrange("p (k o) -> p k o", o=1).to_broadcast([128, 4, TP])
                    L.tell(tt(feat[:, 4 * j:4 * j + 4, TP * i:TP * i + TP], src, w, ALU.mult), "feat_ready", 2 * i + j + 1)
            dve.sem_inc(sg["bank_free"], 4)
            dve.wait_ge(sg["lb_exp"], 1)
            L(tt(smx[:, 0, 0:H], lbt, omlb, ALU.add))
            L(v.reciprocal(smx[:, 0, 0:H], smx[:, 0, 0:H]))
            L(tt(lbt, lbt, smx[:, 0, 0:H], ALU.mult))
            L(ts(omlb, lbt, -1.0, 1.0, ALU.mult, ALU.add))
            dve.wait_ge(*mark["ab_done"])
            L.tell(v.tensor_copy(ab, bank(0)[0:TP, 0:24].rearrange("p (i h) -> p i h", i=NI)), "ab_taken")
            dve.wait_ge(sg["par_in"], 32)
            dtb3 = dtb.rearrange("p (o h) -> p o h", o=1).to_broadcast([TP, NI, H])
            alb3 = alb.rearrange("p (o h) -> p o h", o=1).to_broadcast([TP, NI, H])
            L(tt(Gt, ab[:, :, 0:H], dtb3, ALU.add))
            L(ts(gt, Gt, 0.0, None, ALU.max))
            L(ts(Gl, Gt, -1.0, None, ALU.mult))
            L.tell(tt(Gl, Gt, Gl, ALU.min), "g_pre")
            dve.wait_ge(sg["g_exp"], 1)
            L(tt(gt, gt, Gl, ALU.add))
            L(tt(gt, gt, alb3, ALU.mult))
            L(ts(gt, gt, -1.0, None, ALU.mult))
            dve.wait_ge(sg["beta_sig"], 1)
            L(v.tensor_copy(btm, bt))
            L.tell(v.memset(btm[0:LEAD, 0, :], 0.0), "g_ready")
            dve.wait_ge(sg["bank_free"], 4 + KB_ + 2 * H)
            raw = proj[:, QB_:QB_ + FC, :]
            L(v.tensor_copy(conv_pack[:, :, 0:NS], raw[:, :, 0:NS]))
            L.tell(v.tensor_copy(conv_pack[:, :, NS:NS + 3], raw[:, :, T - 3:T]), "conv_packed")
            cw = lambda j: prmT[:, 16 + FC * j:16 + FC * j + FC].rearrange("p (f o) -> p f o", o=1).to_broadcast([128, FC, NS])
            L(tt(smx, conv_pack[:, :, 0:NS], cw(CW - 1), ALU.mult))
            for j in range(CW - 1):
                L(tt(smy, bufT[:, :, :, j], cw(j), ALU.mult))
                L(tt(smx, smx, smy, ALU.add))
            for g in range(3):
                cvg = cv[g].rearrange("p (h t) -> p h t", h=H)
                L(v.memset(cvg[:, :, NS:LEAD], 0.0))
                L(v.tensor_copy(cvg[:, :, 0:NS], smx[:, H * g:H * g + H, :]))
                for h in range(H):
                    fi = H * g + h
                    L(ts(cvg[:, h, LEAD:T], raw[:, fi, LEAD:T], prmT[:, 16 + FC * (CW - 1) + fi:17 + FC * (CW - 1) + fi],
                         None, ALU.mult))
                    for s in range(1, CW):
                        w = prmT[:, 16 + FC * (CW - 1 - s) + fi:17 + FC * (CW - 1 - s) + fi]
                        L(stt(out=cvg[:, h, LEAD + s:T], in0=raw[:, fi, LEAD:T - s], scalar=w, in1=cvg[:, h, LEAD + s:T],
                              op0=ALU.mult, op1=ALU.add))
                dve.sem_inc(sg["conv_out"], 1)
            dve.wait_ge(sg["a_sig"], 3)
            dve.wait_ge(sg["bank_free"], 4 + NFT)
            L(stt(out=flat(Q_), in0=flat(Q_), scalar=SCALE, in1=W0, op0=ALU.mult, op1=ALU.mult))
            for h in range(H):
                L(ts(wideh(1)[:, h, :], wideh(1)[:, h, :], omlb[:, h:h + 1], lbt[:, h:h + 1], ALU.mult, ALU.add))
            L(tt(wideh(2), wideh(2), omlb.rearrange("p (h o) -> p h o", o=1).to_broadcast([128, H, T]), ALU.mult))
            L(v.tensor_copy(smf, wideh(1)[:, :, 0:NS]))
            L(v.tensor_copy(smk, wideh(2)[:, :, 0:NS]))
            L.tell(v.tensor_copy(smq, group(Q_)[:, :, 0:NS]), "a_fg")
            dve.wait_ge(sg["a_ln"], 1)
            for h in range(H):
                L(v.tensor_tensor_scan(wideh(1)[:, h, :], keep[:], proj[:, F_ + h, :], 0.0, ALU.mult, ALU.add))
            chunked = lambda a: a.rearrange("p (n t) -> p n t", t=C)
            NN = HT // C
            L.tell(tt(chunked(flat(F_)), chunked(W1), chunked(W1)[:, :, C // 2 - 1:C // 2].to_broadcast([128, NN, C]),
                      ALU.subtract), "a_diff")
            dve.wait_ge(sg["a_exp"], 2)
            L.tell(tt(W0, flat(Q_), W0, ALU.mult), "scA_ops", 1)
            L.tell(tt(flat(F_), W2, flat(F_), ALU.mult), "scA_ops", 2)
            dve.wait_ge(sg["a_expb"], 1)
            L(v.tensor_copy(decA, group(I_).rearrange("p h (n t) -> p h n t", t=C)[:, :, :, C - 1]))
            L(tt(flat(I_), flat(Q_), flat(I_), ALU.mult))
            L.tell(tt(chunked(flat(Q_)), chunked(W1)[:, :, C - 1:C].to_broadcast([128, NN, C]), chunked(W1), ALU.subtract),
                   "a_kdiff")
            dve.wait_ge(sg["vA_taken"], 1)
            L(v.memset(vtA[0:LEAD, 0], 0.0))
            dve.wait_ge(sg["a_kexp"], 1)
            L.tell(tt(flat(Q_), W2, flat(Q_), ALU.mult), "kA_ready")
            bc = lambda m: m[:].rearrange("p (o t) -> p o t", o=1).to_broadcast([TP, NI * H, C])
            m12 = lambda a: a.rearrange("p i h t -> p (i h) t")
            dve.wait_ge(*mark["scA_done"])
            L.tell(tt(m12(PT), bank(7)[0:TP, 0:NI * H * C].rearrange("p (n t) -> p n t", t=C), bc(causal), ALU.mult),
                   "PT_ready")
            for g in range(3):
                dve.wait_ge(sg["conv_sig"], g + 1)
                L.tell(tt(flat(QB_ + H * g), flat(QB_ + H * g), cv[g], ALU.mult), "conv_done", g + 1)
            dve.wait_ge(sg["l2_root"], 1)
            L(v.reciprocal(cv[0], cv[0]))
            L(stt(out=flat(QB_), in0=flat(QB_), scalar=SCALE, in1=cv[0], op0=ALU.mult, op1=ALU.mult))
            L.tell(v.tensor_copy(gmq, group(QB_)[:, :, 0:NS]), "b_normed", 1)
            dve.wait_ge(sg["l2_root"], 2)
            L(v.reciprocal(cv[1], cv[1]))
            L(tt(flat(KB_), flat(KB_), cv[1], ALU.mult))
            L.tell(v.tensor_copy(gmk, group(KB_)[:, :, 0:NS]), "b_normed", 2)
            dve.wait_ge(*mark["cum_done"])
            L(v.tensor_copy(Gt, bank(3)[0:TP, 0:12].rearrange("p (i h) -> p i h", i=NI)))
            L.tell(v.tensor_copy(Gl, bank(3)[0:TP, 16:28].rearrange("p (i h) -> p i h", i=NI)), "G_taken")
            L(tt(eGl, Gl, Gt, ALU.subtract))
            dve.wait_ge(sg["G_exps"], 2)

            def chunk_cols(b0, c):
                a = ps[C * c:C * c + C, b0:b0 + H, 0:T].rearrange("p h (i t) -> p i h t", i=NI)
                return a[:, :, :, C * c:C * c + C]

            for c in range(NCC):
                rows = slice(C * c, C * c + C)
                for i in range(NI):
                    ins = tt(LT[rows, i], chunk_cols(4, c)[:, i],
                             Gt[rows, i, :].rearrange("p (h o) -> p h o", o=1).to_broadcast([C, H, C]), ALU.subtract)
                    L(ins)
                dve.sem_inc(sg["G_diffs"], 1)
            L.tell(ts(LT, LT, 0.0, None, ALU.min), "lt_diff")
            L(v.tensor_copy(sbbeta, ps[:, 0:H, 0:NS]))
            dve.wait_ge(sg["lt_exp"], 3)
            L(tt(m12(LT), m12(LT), bc(causal), ALU.mult))
            L(tt(bG, bG, btm, ALU.mult))
            dve.wait_ge(*mark["scB_done"])
            prod = psf[0:TP, 2048:2048 + 768].rearrange("p (n t) -> p n t", t=2 * C)
            L(tt(m12(AT), prod[:, :, 0:C], m12(LT), ALU.mult))
            L(tt(m12(MT), prod[:, :, C:2 * C], m12(LT), ALU.mult))
            L(tt(m12(MT), m12(MT), bc(strict), ALU.mult))
            for c in range(NCC):
                rows = slice(C * c, C * c + C)
                for i in range(NI):
                    L(tt(MT[rows, i], chunk_cols(0, c)[:, i], MT[rows, i], ALU.mult))
            dve.sem_inc(mark["MT_ready"][0], 1)
            dve.wait_ge(sg["G_exps"], 1)
            L.tell(tt(flat(QB_), flat(QB_), W0, ALU.mult), "qdec_ready")
            heads = lambda b: bank(b)[0:TP, :].rearrange("p (h n) -> p h n", h=H)
            per_head = lambda a, i: a[:, i, :].rearrange("p (h o) -> p h o", o=1).to_broadcast([TP, H, DK])
            tb = (6, 7, 3)
            for i in range(NI):
                dve.wait_ge(sg["kB_turned"], i + 1)
                L(tt(kbe[:, i], heads(tb[i]), per_head(bG, i), ALU.mult))
                L.tell(tt(kdB[:, i], heads(tb[i]), per_head(eGl, i), ALU.mult), "kB_taken", i + 1)
            for i in range(NI):
                dve.wait_ge(sg["vB_turned"], i + 1)
                L.tell(tt(vb[:, i], heads(tb[i]), per_head(btm, i), ALU.mult), "vB_taken", i + 1)

            def write_states(spread, done, key, base):
                for b in range(NS):
                    dve.wait_ge(sg[spread], b + 1)
                    for h in range(H):
                        stt(out=states[:, H * b + h, :], in0=bank(b % 2)[:, 128 * h:128 * h + 128], scalar=key[:, h, b:b + 1],
                            in1=states[:, H * b + h, :], op0=ALU.mult, op1=ALU.add).then_inc(sg[done], 1)
                    dve.wait_ge(sg[done], H * b + H)
                    dve.sem_inc(sg["spread_used"], 1)

            dve.wait_ge(sg["stA_decayed"], 1)
            write_states("stA_spread", "stA_new", smk, 0)
            dve.wait_ge(sg["pair_in"], 16)
            dve.wait_ge(sg["pairX_one"], 1)
            for j in range(C - 1):
                n, m = j + 1, C - 1 - j
                wv = pairW[:, 0:n * m].rearrange("p (s t) -> p s t", s=n)
                L(tt(wv, pairX[:, 0:n, j:j + 1].to_broadcast([NP, n, m]), pairM[:, j:j + 1, j + 1:C].to_broadcast([NP, n, m]),
                     ALU.mult))
                L(tt(pairX[:, 0:n, j + 1:C], pairX[:, 0:n, j + 1:C], wv, ALU.subtract))
            dve.sem_inc(mark["inv_ready"][0], 1)
            dve.wait_ge(*mark["stB_kS"])
            L(tt(sdelta, proj[:, VB_:VB_ + H, 0:NS], bank(2)[:, 0:H * NS].rearrange("p (h b) -> p h b", h=H), ALU.subtract))
            L.tell(tt(sdelta, sdelta, sbbeta, ALU.mult), "stB_delta")
            write_states("stB_spread", "stB_new", gmk, NS)
            for n in range(NI * NCC):
                i, c = n // NCC, n % NCC
                end = TP * i + C * c + C - 1
                dve.wait_ge(sg["kvA_done"], n + 1)
                if n == 0:
                    L(v.tensor_copy(spA, bank(2).rearrange("p (h v) -> p h v", h=H)))
                    dve.wait_ge(sg["stepB_done"], 1)
                    L(v.tensor_copy(spB, bank(5).rearrange("p (h v) -> p h v", h=H)))
                else:
                    for h in range(H):
                        L(stt(out=spA[:, h, :], in0=spA[:, h, :], scalar=decA[:, h, n:n + 1],
                              in1=bank(2)[:, 128 * h:128 * h + 128], op0=ALU.mult, op1=ALU.add))
                    dve.wait_ge(sg["stepB_done"], n + 1)
                    for h in range(H):
                        L(stt(out=spB[:, h, :], in0=spB[:, h, :], scalar=wideh(0)[:, h, end:end + 1],
                              in1=bank(5)[:, 128 * h:128 * h + 128], op0=ALU.mult, op1=ALU.add))
                dve.sem_inc(sg["state_upd"], 1)
            for g, (out, sig, o, w) in enumerate(((G_, F_, Q_, 64), (Z_, VB_, KB_, 65))):
                dve.wait_ge(sg["n_sig"], g + 1)
                L(tt(flat(out), flat(out), flat(sig), ALU.mult))
                dve.wait_ge(sg["n_root"], g + 1)
                L(v.reciprocal(wide[:, g, :], wide[:, g, :]))
                L(tt(flat(out), flat(out), wide[:, g, :], ALU.mult))
                L.tell(stt(out=flat(out), in0=flat(out), scalar=prmT[:, w:w + 1], in1=flat(o), op0=ALU.mult, op1=ALU.mult),
                       "ya_ready", g + 1)
            dve.wait_ge(sg["gates_sig"], 1)
            dve.wait_ge(sg["conv_stored"], 48)
            for m in range(KT):
                t0, t1 = proj[:, VB_, :], proj[:, VB_ + 1, :]
                dve.wait_ge(sg["oab_done"], m + 1)
                L(tt(t0, bank(2 * (m % 4))[:, 0:T], proj[:, GA_ + m, :], ALU.mult))
                L.tell(tt(t1, bank(2 * (m % 4) + 1)[:, 0:T], proj[:, GB_ + m, :], ALU.mult), "proj_out_used", m + 1)
                L.tell(tt(feat[:, m, :], t0, t1, ALU.add), "merged_ready", m + 1)
            for i in range(NI):
                for j in range(2):
                    dve.wait_ge(sg["mix_done"], 2 * i + j + 1)
                    L.tell(tt(x_tok[:, i, 512 * j:512 * j + 512], x_tok[:, i, 512 * j:512 * j + 512],
                              bank(2 * i + j)[0:TP, :], ALU.add), "x2_ready", 2 * i + j + 1)
            dve.wait_ge(sg["nffn_in"], 16)
            for i in range(NI):
                dve.wait_ge(sg["x2_summed"], i + 1)
                L(v.reciprocal(rstd[:, i:i + 1], rstd[:, i:i + 1]))
                L.tell(stt(out=x2h[:, i, :], in0=x_tok[:, i, :], scalar=rstd[:, i:i + 1], in1=nffn_b,
                           op0=ALU.mult, op1=ALU.mult), "x2_normed", i + 1)
            dve.wait_ge(*mark["logits_done"])
            dve.wait_ge(sg["route_in"], 32)
            dve.wait_ge(sg["route_consts"], 1)
            L(tt(lg, bank(4)[0:TP, 0:NI * NE].rearrange("p (i e) -> p i e", i=NI),
                 br_b.rearrange("p (o e) -> p o e", o=1).to_broadcast([TP, NI, NE]), ALU.add))
            for i in range(NI):
                L(v.max(m8[:, i, :], lg[:, i, :]))
                L(v.max_index(i8[:, i, :], m8[:, i, :], lg[:, i, :]))
            L(v.tensor_copy(i8f, i8))
            for i in range(NI):
                for j in range(TOP_K):
                    L(ts(oneh[:, i, j, :], iota_e, i8f[:, i, j:j + 1], None, ALU.is_equal))
            L(tt(selm, oneh[:, :, 0, :], oneh[:, :, 1, :], ALU.add))
            L(tt(selm, selm, oneh[:, :, 2, :], ALU.add))
            L(tt(selm, selm, oneh[:, :, 3, :], ALU.add))
            L(tt(gate, m8[:, :, 0:TOP_K], m8[:, :, 0:1].to_broadcast([TP, NI, TOP_K]), ALU.subtract))
            L(ts(dump, dump, hole, None, ALU.mult))
            L(ts(hole, hole, -1.0, 1.0, ALU.mult, ALU.add))
            L(ts(oneh[:, 0], oneh[:, 0], hole, None, ALU.mult))
            L.tell(ts(selm[:, 0, :], selm[:, 0, :], hole, None, ALU.mult), "sel_done")
            dve.wait_ge(sg["top_exp"], 1)
            L(v.tensor_reduce(gsum, gate, AX.X, ALU.add))
            L(v.reciprocal(gsum, gsum))
            L(tt(gate, gate, gsum.rearrange("p (i o) -> p i o", o=1).to_broadcast([TP, NI, TOP_K]), ALU.mult))
            dve.wait_ge(*mark["cnt_done"])
            cnt_c, ext = extc[:, 1:2], extc[:, 0:1]
            L(v.tensor_copy(cnt_c, bank(6)[0:NE, 0:1]))
            L(ts(ext, cnt_c, float(CAP), None, ALU.is_gt))
            n = 2 * CAP
            while n < T:
                L(ts(sel4[0:NE, 0:1], cnt_c, float(n), None, ALU.is_gt))
                L(tt(ext, ext, sel4[0:NE, 0:1], ALU.add))
                n += CAP
            dve.sem_inc(mark["ext_ready"][0], 1)
            dve.wait_ge(*mark["off_done"])
            L(v.tensor_copy(offc[:, 0:1], bank(6)[0:NE, 8:9]))
            L(tt(offc[:, 1:2], offc[:, 0:1], ext, ALU.add))
            L(ts(nblk, bank(6)[0:1, 16:17], float(NE), None, ALU.add))
            L(v.tensor_copy(nbi, nblk))
            L(ts(offx, bank(6)[0:TP, 64:64 + NE], float(NE - 1), None, ALU.add))
            L(tt(offx, offx, iota_e, ALU.subtract))
            L(v.tensor_copy(slot, bank(5)[0:TP, 0:NI * NE].rearrange("p (i e) -> p i e", i=NI)))
            L(ts(rtmp, slot, float(CAP), None, ALU.is_ge))
            b3 = lambda a: a.rearrange("p (o e) -> p o e", o=1).to_broadcast([TP, NI, NE])
            L(tt(rtmp, rtmp, b3(offx), ALU.mult))
            L(tt(rtmp, rtmp, b3(iota_e), ALU.add))
            L(stt(out=slot, in0=rtmp, scalar=float(CAP), in1=slot, op0=ALU.mult, op1=ALU.add))
            for j in range(TOP_K):
                L(tt(rtmp, oneh[:, :, j, :], slot, ALU.mult))
                L(v.tensor_reduce(slotf[:, :, j:j + 1].rearrange("p i o -> p (i o)"), rtmp, AX.X, ALU.add))
            L(v.tensor_copy(sloti, slotf))
            for j in range(TOP_K):
                L(ts(slotf[:, 0, j:j + 1], slotf[:, 0, j:j + 1], dump[:, j:j + 1], None, ALU.add))
            L.tell(v.tensor_copy(slotw, slotf), "slot_ready")
            L(ts(eh, iota_b, iota_p, None, ALU.is_equal))
            L(ts(iota_b, iota_b, -float(NE), None, ALU.add))
            L(ts(ehx, iota_b, offc[:, 0:1], None, ALU.is_ge))
            L(ts(iota_b, iota_b, offc[:, 1:2], None, ALU.is_lt))
            L(tt(ehx, ehx, iota_b, ALU.mult))
            L(tt(eh, eh, ehx, ALU.add))
            for p in range(2):
                L(v.tensor_copy(eh3[NE * p:NE * p + NE], eh))
            L.tell(v.tensor_copy(eh3[2 * NE:3 * NE], eh), "eh_ready")
            dve.wait_ge(*mark["blk_done"])
            L(v.tensor_copy(blke, bank(6)[0:1, 128:128 + NBT]))
            dve.sem_inc(mark["nb_ready"][0], 1)
            dve.wait_ge(*mark["tok_turned"])
            L.tell(v.tensor_copy(tokT, bank(7)[0:CAP, 0:NBT]), "tokT_ready")
            dve.wait_ge(*mark["nb_ready"])
            nb = dve.value_load(nbi[0:1, 0:1], min_val=NE, max_val=NBX)
            rows_T = bank(2).rearrange("p (k t) -> p k t", k=KT)
            dve.wait_ge(sg["xg_turned"], 1)
            v.tensor_copy(xgT, rows_T).then_inc(sg["xg_ready"], 1)
            dve.sem_inc(sg["up_clipped"], 1)
            with dve.Fori(0, nb) as b:
                dve.wait_ge(sg["gu_used"], KT * b + KT)
                ts(hid_g, bank(0), SWIGLU_LIMIT, None, ALU.min).then_inc(sg["gate_clipped"], 1)
                ts(hid_u, bank(1), SWIGLU_LIMIT, -SWIGLU_LIMIT, ALU.min, ALU.max).then_inc(sg["up_clipped"], 1)
                dve.wait_ge(sg["gate_clipped"], b + 1)
                dve.wait_ge(sg["up_clipped"], b + 2)
                stt(out=hid_u, in0=hid_u, scalar=1.0, in1=hid_g, op0=ALU.add, op1=ALU.mult).then_inc(sg["gu_mult"], 1)
                dve.wait_ge(sg["gu_mult"], b + 1)
                dve.wait_ge(sg["sig_ready"], b + 1)
                tt(hid, hid_u, hid_s, ALU.mult).then_inc(sg["hid_ready"], 1)
                dve.wait_ge(sg["xg_turned"], b + 2)
                v.tensor_copy(xgT, rows_T).then_inc(sg["xg_ready"], 1)
            for i in range(NI):
                dve.wait_ge(sg[f"yg_in{i}"], 16 * TOP_K)
                for j in range(TOP_K):
                    L(stt(out=x_tok[:, i, :], in0=y_rows[i][j], scalar=gate[:, i, j:j + 1], in1=x_tok[:, i, :],
                          op0=ALU.mult, op1=ALU.add))
                dve.sem_inc(sg["yg_summed"], 1)
            dve.wait_ge(sg["nfin_in"], 16)
            for i in range(NI):
                dve.wait_ge(sg["f_summed"], i + 1)
                L(v.reciprocal(rstd[:, i:i + 1], rstd[:, i:i + 1]))
                L.tell(stt(out=x_tok[:, i, :], in0=x_tok[:, i, :], scalar=rstd[:, i:i + 1], in1=nfin_b,
                           op0=ALU.mult, op1=ALU.mult), "f_ready", i + 1)


_INS = ["x_prompt", "x_sample", "state_hgrn", "state_gdn", "state_conv", "meta_tokens", "lb_param", "norm_mix",
        "w_in", "conv_w", "a_log", "dt_bias", "hgrn_norm_w", "gdn_norm_w", "w_oa", "w_ob", "w_out", "norm_ffn",
        "w_router", "b_router", "w_gu", "b_gu", "w_down", "b_down", "norm_final"]


def kernel(**inputs):
    import numpy as _np
    import concourse.bacc as _bacc
    from concourse import mybir as _mybir
    from concourse.bass_utils import run_bass_kernel_spmd as _run

    nc = _bacc.Bacc("TRN2", target_bir_lowering=False, num_devices=1)
    arrays, args = {}, []
    for name in _INS:
        a = _np.ascontiguousarray(inputs[name])
        arrays[f"in_{name}"] = a
        args.append(nc.dram_tensor(f"in_{name}", a.shape, _mybir.dt.from_np(a.dtype), kind="ExternalInput").ap())
    shape = {n: inputs[n].shape for n in _INS}
    batch = shape["x_prompt"][0]
    outs = [shape["x_prompt"], shape["x_sample"],
            (shape["state_hgrn"][0], batch) + tuple(shape["state_hgrn"][2:]),
            (shape["state_gdn"][0], batch) + tuple(shape["state_gdn"][2:]),
            (shape["state_conv"][0], batch) + tuple(shape["state_conv"][2:]),
            shape["state_hgrn"], shape["state_gdn"], shape["state_conv"]]
    for i, s in enumerate(outs):
        args.append(nc.dram_tensor(f"out_{i}", tuple(s), _mybir.dt.float32, kind="ExternalOutput").ap())
    hybrid_decoder_step(nc, *args)
    r = _run(nc, [arrays], core_ids=[0])
    return tuple(r.results[0][f"out_{i}"] for i in range(len(outs)))
```

```python
import concourse.bass as bass
from concourse import mybir
from contextlib import ExitStack

F32 = mybir.dt.float32
BF16 = mybir.dt.bfloat16
I32 = mybir.dt.int32
U32 = mybir.dt.uint32
ALU = mybir.AluOpType
ACT = mybir.ActivationFunctionType
AX = mybir.AxisListType

RMS_EPS = 1e-6
L2_EPS = 1e-6
SWIGLU_LIMIT = 7.0
SWIGLU_ALPHA = 1.702
TOP_K = 4


def hybrid_decoder_step(nc, x_prompt, x_sample, state_hgrn, state_gdn, state_conv, meta_tokens, lb_param,
                        norm_mix, w_in, conv_w, a_log, dt_bias, hgrn_norm_w, gdn_norm_w, w_oa, w_ob, w_out,
                        norm_ffn, w_router, b_router, w_gu, b_gu, w_down, b_down, norm_final,
                        y_prompt, y_sample, hgrn_prompt, gdn_prompt, conv_prompt,
                        hgrn_sample, gdn_sample, conv_sample):
    _, SEQ, D = x_prompt.shape
    NS = x_sample.shape[0]
    NM = meta_tokens.shape[0]
    _, _, H, DK, DV = state_hgrn.shape
    CW = conv_w.shape[1]
    DC = state_conv.shape[3]
    NE = w_gu.shape[1]
    KT = D // 128
    FC = DC // 128
    LEAD = 16
    T = LEAD + NM + SEQ
    TP = 96
    NI = T // TP
    C = 32
    NCC = TP // C
    HT = H * T
    CAP = 64
    NBX = NE + (T * TOP_K) // CAP
    NBT = NBX + 1
    SCALE = float(DK) ** -0.5
    HF = D // 2
    AB0 = 4 * H * DK + DC
    WCH = 512
    NCHUNK = (w_in.shape[2] - 2 * H) // WCH
    NRING = 3
    Q_, F_, I_, G_, QB_, KB_, VB_, Z_, GA_, GB_ = 0, 4, 8, 12, 16, 20, 24, 28, 32, 40
    NFT = 48
    ORDER = [4, 5, 6, 0, 1, 2, 3, 7, 8, 9, 10, 11]
    FILL = (33, 35, 36, 38, 39, 41, 42, 44, NFT)
    NEARLY = 24
    SMALL = 880
    DOWN0 = 8

    ctx = ExitStack()
    with ctx:
        def sb(name, shape, dt=F32):
            return ctx.enter_context(nc.sbuf_tensor(name, shape, dt))

        def sem(name):
            return ctx.enter_context(nc.semaphore(name))

        def dram(name, shape, dt=F32):
            return nc.dram_tensor(name, shape, dt, kind="Internal").ap()

        ring = sb("ring", [128, 12, 2048])
        proj = sb("proj", [128, NFT, T])
        states = sb("states", [128, NS * H, DV])
        x_tok = sb("x_tok", [TP, NI, D])
        feat = sb("feat", [128, KT, T])
        wide = sb("wide", [128, 3, HT])
        ident = sb("ident", [128, 128])
        ones = sb("ones", [128, 128])
        tri = sb("tri", [TP, NCC, C])
        same = sb("same", [TP, NCC, C])
        causal = sb("causal", [TP, C])
        strict = sb("strict", [TP, C])
        keep = sb("keep", [128, T], BF16)
        w_ab = sb("w_ab", [128, KT, 2 * H])
        w_rt = sb("w_rt", [128, KT, NE])
        sm = sb("sm", [128, SMALL])
        epsb = sb("epsb", [128, 1])

        ringf = ring[:].rearrange("p s n -> p (s n)")
        win_buf = [ringf[:, 4096 * j:4096 * (j + 1)].rearrange("p (k n) -> p k n", k=KT) for j in range(NRING)]
        woa_sb = ringf[:, 0:4096].rearrange("p (k n) -> p k n", k=H)
        wob_sb = ringf[:, 4096:8192].rearrange("p (k n) -> p k n", k=H)
        wout_lo = ringf[:, 8192:12288].rearrange("p (k n) -> p k n", k=H)
        statesf = states[:].rearrange("p s n -> p (s n)")
        wout_hi = statesf.rearrange("p (k n) -> p k n", k=H)
        work = ringf[:, 12288:24576]

        def wk(at, n, parts=128):
            return work[0:parts, at:at + n]

        def tokmaj(at):
            return wk(at, 1536, TP).rearrange("p (i h n) -> p i h n", i=NI, h=H)

        kdA, vtA, kbe, kdB, vb = (tokmaj(1536 * j) for j in range(5))

        def blocks(at):
            return wk(at, 384, TP).rearrange("p (i h t) -> p i h t", i=NI, h=H)

        PT, LT, AT, MT, XT = (blocks(7680 + 384 * j) for j in range(5))
        NP = NI * NCC * H
        pairM = wk(9600, C * C, NP).rearrange("p (s t) -> p s t", s=C)
        pairX = wk(10624, C * C, NP).rearrange("p (s t) -> p s t", s=C)
        pairW = wk(11648, 256, NP)
        v_new = wk(9600, H * DV, TP)
        prm_rows = wk(4608, 128, 66)
        bufT = wk(11904, FC * NS * (CW - 1)).rearrange("p (f b j) -> p f b j", f=FC, b=NS)
        xh = wk(0, NI * D, TP).rearrange("p (i d) -> p i d", i=NI)
        buf_rows = wk(3072, DC, NS * (CW - 1))
        featf = feat[:].rearrange("p k t -> p (k t)")
        v_row = work[64:64 + NS, 10624:10624 + H * DV]
        conv_new = work[96:96 + NS + 3, 9600:9600 + DC]
        decB = wide[:, 2, 1024:1024 + H * NI * NCC].rearrange("p (h c) -> p h c", h=H)
        xnT = proj[:, GA_:GA_ + KT, :]
        projf = proj[:].rearrange("p f t -> p (f t)")
        b_f32 = projf[0:3 * NE, 0:3 * D]
        hid_g, hid_u, hid_s, hid = (projf[:, 3072 + 512 * j:3584 + 512 * j] for j in range(4))
        hidT = projf[:, 5120:5632].rearrange("p (c t) -> p c t", c=4)
        y_out = projf[:, 5632:6144]
        xg = projf[0:CAP, 6144:7168]
        xgT = projf[:, 7168:7680].rearrange("p (k t) -> p k t", k=KT)
        sel_gu = projf[0:3 * NE, 7680:7680 + CAP // 2].bitcast(BF16)
        sel_dn = projf[0:3 * NE, 7712:7712 + CAP // 2].bitcast(BF16)
        nfin_b = projf[0:TP, 7744:7744 + D]
        nffn_b = projf[0:TP, 11520:11520 + D]
        x2h = statesf[0:TP, 0:NI * D].rearrange("p (i d) -> p i d", i=NI)
        spA, spB = (wide[:, 2, 512 * j:512 * j + 512].rearrange("p (h v) -> p h v", h=H) for j in range(2))
        cv = [wk(3072 + 1536 * g, HT) for g in range(3)]
        y_rows = [[ringf[0:TP, D * (TOP_K * i + j):D * (TOP_K * i + j) + D] for j in range(TOP_K)] for i in range(NI)]
        W0, W1, W2 = (wide[:, j, :] for j in range(3))
        wideh = lambda j: wide[:, j, :].rearrange("p (h t) -> p h t", h=H)

        at = [0]

        def small(n, dt=F32, parts=128):
            a = sm[0:parts, at[0]:at[0] + n]
            at[0] += n
            assert at[0] <= SMALL
            return a.bitcast(dt) if dt != F32 else a

        prmT = small(66)
        lbt, omlb = small(H), small(H)
        smq, smk, smf, gmq, gmk = (small(H * NS).rearrange("p (h b) -> p h b", h=H) for _ in range(5))
        sbeg, sbbeta, sdelta = (small(H * NS).rearrange("p (h b) -> p h b", h=H) for _ in range(3))
        decA = small(H * NI * NCC).rearrange("p (h c) -> p h c", h=H)
        ab = small(24, parts=TP).rearrange("p (i h) -> p i h", i=NI)
        gt, bt, Gt, Gl, bG, eGl, btm = (small(12, parts=TP).rearrange("p (i h) -> p i h", i=NI) for _ in range(7))
        alb, dtb = small(H, parts=TP), small(H, parts=TP)
        ss, rstd = small(NI, parts=TP), small(NI, parts=TP)
        conv_pack = small(FC * (NS + 3)).rearrange("p (f c) -> p f c", f=FC)
        smx, smy = (small(FC * NS).rearrange("p (f b) -> p f b", f=FC) for _ in range(2))
        soA, soB = (small(H * NS).rearrange("p (h b) -> p h b", h=H) for _ in range(2))
        nbi = small(1, I32, 1)
        tkc = small(1, I32, CAP)
        rt = [0]
        wr = wide[:].rearrange("p a n -> p (a n)")

        def rsmall(n, dt=F32, parts=TP):
            a = wr[0:parts, rt[0]:rt[0] + n]
            rt[0] += n
            assert rt[0] <= 3 * HT
            return a.bitcast(dt) if dt != F32 else a

        br_b = rsmall(NE)
        lg = rsmall(NI * NE).rearrange("p (i e) -> p i e", i=NI)
        selm = rsmall(NI * NE).rearrange("p (i e) -> p i e", i=NI)
        slot = rsmall(NI * NE).rearrange("p (i e) -> p i e", i=NI)
        rtmp = rsmall(NI * NE).rearrange("p (i e) -> p i e", i=NI)
        oneh = rsmall(NI * TOP_K * NE).rearrange("p (i j e) -> p i j e", i=NI, j=TOP_K)
        m8 = rsmall(NI * 8).rearrange("p (i e) -> p i e", i=NI)
        i8 = rsmall(NI * 8, U32).rearrange("p (i e) -> p i e", i=NI)
        i8f = rsmall(NI * 8).rearrange("p (i e) -> p i e", i=NI)
        gate = rsmall(NI * TOP_K).rearrange("p (i e) -> p i e", i=NI)
        gsum = rsmall(NI)
        slotf = rsmall(NI * TOP_K).rearrange("p (i e) -> p i e", i=NI)
        sloti = rsmall(NI * TOP_K, I32).rearrange("p (i e) -> p i e", i=NI)
        slotw = rsmall(NI * TOP_K, I32).rearrange("p (i e) -> p i e", i=NI)
        iota_e = rsmall(NE)
        expb = rsmall(NE)
        cnt = rsmall(NE)
        extra = rsmall(NE)
        offs = rsmall(NE)
        offx = rsmall(NE)
        tokid = rsmall(NI)
        triT = rsmall(TP)
        iota_b = rsmall(NBT, parts=NE)
        eh = rsmall(NBT, parts=NE)
        offc = rsmall(2, parts=NE)
        ehx = rsmall(NBT, parts=NE)
        eh3 = rsmall(NBT, parts=3 * NE)
        b3 = rsmall(3 * D // 2, parts=3 * NE).bitcast(BF16)
        lower = rsmall(2, parts=3 * NE)
        blke = rsmall(NBT, I32, 1)
        blkf = rsmall(NBT, parts=1)
        nblk = rsmall(1, parts=1)
        iota_p = rsmall(1, parts=NE)
        tokT = rsmall(NBT, I32, CAP)
        tok_rows = rsmall(CAP, parts=NBT)
        hole, dump = rsmall(1), rsmall(TOP_K)
        extc = rsmall(2, parts=NE)
        sel4 = rsmall(NE)

        ps = ctx.enter_context(nc.psum_tensor("ps", [128, 8, 512], F32))
        psf = ps[:].rearrange("p b n -> p (b n)")
        bank = lambda j: ps[:, j, :]

        xn_dram = dram("xn_dram", [T, D])
        y_dram = dram("y_dram", [NBT * CAP, D])
        tok_dram = dram("tok_dram", [NBT * CAP, 1])
        pair_dram = dram("pair_dram", [NP, C, C])
        inv_dram = dram("inv_dram", [NP, C, C])

        sg = {name: sem(name) for name in """
            x_in0 x_in1 x_in2 prm_in buf_in ab_in par_in 
            win_in0 win_in1 win_in2
            consts lead_zero  tok_zeroed y_zeroed pairX_one
            x_summed x_normed x_turned feat_ready   lb_exp  
              ptile_done bank_free
            a_sig  a_ln  a_exp a_expb  a_kexp  vA_turned vA_taken scA_ops  
             kA_turned kA_taken
            conv_out conv_sig conv_done sq_ready l2_done l2_root b_normed  
             g_exp  beta_sig     lt_exp  G_diffs G_exps
             pair_stored pair_in  inv_stored XT_in
            kB_turned kB_taken vB_turned vB_taken  wT_taken 
            stepA_done oA_taken stateA_upd solve_step silu_done oa_done oa_gated
            vnew_done vnew_taken kvB_done oB_done oB_taken stateB_upd
            stA_in stB_in stA_decayed stB_decayed stA_spread stA_new     stB_row
            stB_spread stB_new  oA_sample oB_sample stA_stored stB_stored spread_used
              conv_rows conv_stored prompt_stored
            n_sq n_sum n_root n_sig ya_ready gates_sig
            woa_in wob_in wout_in wout2_in  proj_out_used merged_ready oab_done mix_done x2_ready
            x2_summed x2_normed x2_turned xnT_ready  route_in nffn_in bias_in nfin_in
            route_consts top_exp        
            tok_scattered tok_back   xn_stored
            gu_used down_used wait_passed idx_ready xg_in xg_turned xg_ready sel_gu_ready sel_dn_ready b3_ready b3_less
            gate_clipped up_clipped sig_ready gu_mult hid_ready hid_turned hidT_ready y_ready y_stored
            yg_in0 yg_in1 yg_in2 yg_summed f_summed f_ready out_stored
             act_step pool_step dve_step
        """.split()}
        mark = {}
        for owner, names in (("vector_mark", """
                prm_ready lb_diff ab_taken g_pre g_ready conv_packed a_fg G_taken a_diff lt_diff a_kdiff kA_ready PT_ready MT_ready qdec_ready inv_ready stB_delta sel_done ext_ready slot_ready eh_ready nb_ready tokT_ready
                """), ("tensor_mark", """
                prm_turned ab_done cum_done bcast_done conv_turned scA_done scB_done beta_done stA_read stB_kS wT_done stB_turned stB_read logits_done cnt_done off_done blk_done tok_turned
                """)):
            shared = sem(owner)
            mark.update({name: (shared, n + 1) for n, name in enumerate(names.split())})
        w_arrived = [sem(f"w_arrived{j}") for j in range(12)]

        class Steps:

            def __init__(self, eng, name):
                self.eng, self.own, self.count = eng, sg[name], 0

            def __call__(self, ins):
                self.count += 1
                ins.then_inc(self.own, 1)
                self.eng.wait_ge(self.own, self.count)

            def tell(self, ins, name, n=1):
                own, count = mark[name] if name in mark else (sg[name], n)
                ins.then_inc(own, 1)
                self.eng.wait_ge(own, count)

        block = ctx.enter_context(nc.Block())

        @block.sync
        def _(sp):
            sp.dma_start(prm_rows[0:KT, :], norm_mix.rearrange("l (k p) -> (l k) p", p=128)).then_inc(sg["prm_in"], 16)
            sp.dma_start(prm_rows[8:16, :], lb_param.rearrange("r (h p) -> (r h) p", p=128)).then_inc(sg["prm_in"], 16)
            sp.dma_start(prm_rows[16:64, :], conv_w.rearrange("l j (f p) -> (l j f) p", p=128)).then_inc(sg["prm_in"], 16)
            sp.dma_start(prm_rows[64:65, :], hgrn_norm_w).then_inc(sg["prm_in"], 16)
            sp.dma_start(prm_rows[65:66, :], gdn_norm_w).then_inc(sg["prm_in"], 16)
            sp.dma_start(x_tok[:, 1, :], x_prompt[0, 64:160, :]).then_inc(sg["x_in1"], 16)
            sp.dma_start(x_tok[:, 2, :], x_prompt[0, 160:256, :]).then_inc(sg["x_in2"], 16)
            sp.wait_ge(sg["lead_zero"], 1)
            sp.dma_start(x_tok[0:NS, 0, :], x_sample[:, 0, :]).then_inc(sg["x_in0"], 16)
            sp.dma_start(x_tok[LEAD:LEAD + NM, 0, :], meta_tokens).then_inc(sg["x_in0"], 16)
            sp.dma_start(x_tok[LEAD + NM:TP, 0, :], x_prompt[0, 0:64, :]).then_inc(sg["x_in0"], 16)
            sp.dma_start(buf_rows, state_conv[0].rearrange("b j d -> (b j) d")).then_inc(sg["buf_in"], 16)
            sp.dma_start(w_ab[:], w_in[0, :, AB0:AB0 + 2 * H].rearrange("(k p) n -> p k n", p=128)).then_inc(sg["ab_in"], 16)
            def win_load(n):
                c = ORDER[n]
                col = WCH * c + (2 * H if WCH * c >= AB0 else 0)
                if n >= NRING:
                    sp.wait_ge(sg["ptile_done"], 4 * (n - NRING + 1))
                sp.dma_start(win_buf[n % NRING], w_in[0, :, col:col + WCH].rearrange("(k p) n -> p k n", p=128)) \
                    .then_inc(sg[f"win_in{n % NRING}"], 16)

            for n in range(NCHUNK - 1):
                win_load(n)
            sp.wait_ge(*mark["MT_ready"])
            for c in range(NCC):
                sp.dma_start(pair_dram[12 * c:12 * c + 12].rearrange("q s t -> s q t"),
                             MT[C * c:C * c + C].rearrange("s i h t -> s (i h) t")).then_inc(sg["pair_stored"], 16)
            sp.wait_ge(sg["pair_stored"], 16 * NCC)
            sp.dma_start(pairM, pair_dram).then_inc(sg["pair_in"], 16)
            sp.wait_ge(*mark["stA_read"])
            sp.dma_start(hgrn_sample[0].rearrange("b h k v -> k (b h) v"), states[:]).then_inc(sg["stA_stored"], 16)
            sp.wait_ge(sg["stA_stored"], 16)
            sp.dma_start(states[:], state_gdn[0].rearrange("b h k v -> k (b h) v")).then_inc(sg["stB_in"], 16)
            win_load(NCHUNK - 1)
            for n, (w, src, name) in enumerate(((woa_sb, w_oa[0], "woa_in"), (wob_sb, w_ob[0], "wob_in"),
                                                (wout_lo, w_out[0, 0:512, :], "wout_in"))):
                sp.wait_ge(sg["ptile_done"], NFT - 8 + 4 * n)
                sp.dma_start(w, src.rearrange("(k p) n -> p k n", p=128)).then_inc(sg[name], 16)
            sp.wait_ge(*mark["inv_ready"])
            sp.dma_start(inv_dram, pairX).then_inc(sg["inv_stored"], 16)
            sp.wait_ge(sg["inv_stored"], 16)
            for c in range(NCC):
                sp.dma_start(XT[C * c:C * c + C].rearrange("s i h t -> s (i h) t"),
                             inv_dram[12 * c:12 * c + 12].rearrange("q s t -> s q t")).then_inc(sg["XT_in"], 16)
            sp.wait_ge(sg["stateA_upd"], H * NI * NCC)
            sp.dma_start(hgrn_prompt[0, 0].rearrange("h k v -> k h v"), spA).then_inc(sg["prompt_stored"], 16)
            sp.wait_ge(sg["stB_stored"], 16)
            sp.wait_ge(*mark["stB_read"])
            sp.dma_start(wout_hi, w_out[0, 512:1024, :].rearrange("(k p) n -> p k n", p=128)).then_inc(sg["wout2_in"], 16)
            sp.wait_ge(sg["stateB_upd"], H * NI * NCC)
            sp.dma_start(gdn_prompt[0, 0].rearrange("h k v -> k h v"), spB).then_inc(sg["prompt_stored"], 16)
            sp.wait_ge(sg["oab_done"], KT)

            def gu_load(e, k):
                src = w_gu[0, e, 128 * k:128 * k + 128, :] if isinstance(e, int) else \
                    w_gu[0][bass.ds(e, 1), 128 * k:128 * k + 128, :].rearrange("a p n -> (a p) n")
                sp.dma_start(ring[:, k, :], src).then_inc(w_arrived[k], 16)

            def down_load(e, k):
                src = w_down[0, e, 256 * k:256 * k + 256, :] if isinstance(e, int) else \
                    w_down[0][bass.ds(e, 1), 256 * k:256 * k + 256, :].rearrange("a p n -> (a p) n")
                sp.dma_start(ring[:, KT + k, :].rearrange("p (j n) -> p j n", j=2),
                             src.rearrange("(j p) n -> p j n", p=128)).then_inc(w_arrived[KT + k], 16)

            def gu_loads(b, e):
                for k in range(KT):
                    sp.wait_ge(sg["gu_used"], 8 * b - 8 + k + 1)
                    gu_load(e, k)

            def down_loads(b, e):
                for k in range(4):
                    sp.wait_ge(sg["down_used"], DOWN0 + 4 * b - 4 + k + 1)
                    down_load(e, k)

            for k in range(4):
                gu_load(0, k)
            sp.wait_ge(sg["ya_ready"], 2)
            sp.wait_ge(sg["prompt_stored"], 32)
            for k in (6, 7):
                gu_load(0, k)
            sp.wait_ge(sg["mix_done"], 2 * NI)
            for k in (4, 5):
                gu_load(0, k)
            for k in range(4):
                down_load(0, k)
            gu_loads(1, 1)
            with sp.Fori(2, NE) as b:
                gu_loads(b, b)
                down_loads(b - 1, b - 1)
            sp.wait_ge(*mark["nb_ready"])
            nb = sp.value_load(nbi[0:1, 0:1], min_val=NE, max_val=NBX)
            with sp.If(nb > NE):
                with sp.Fori(NE, nb) as b:
                    gu_loads(b, sp.value_load(blke[0:1, bass.ds(b, 1)], min_val=0, max_val=NE - 1))
                    down_loads(b - 1, sp.value_load(blke[0:1, bass.ds(b - 1, 1)], min_val=0, max_val=NE - 1))
            down_loads(nb - 1, sp.value_load(blke[0:1, bass.ds(nb - 1, 1)], min_val=0, max_val=NE - 1))
            sp.wait_ge(sg["prompt_stored"], 32)

        @block.gpsimd
        def _(pool):
            L = Steps(pool, "pool_step")
            gp = nc.gpsimd
            gp.memset(x_tok[0:32, 0, :], 0.0).then_inc(sg["lead_zero"], 1)

            def masked(out, pattern, base, mult, op=ALU.is_ge, fill=0.0):
                L(gp.affine_select(out=out, in_=out, compare_op=op, fill=fill, base=base, pattern=pattern,
                                   channel_multiplier=mult))

            L(gp.memset(ident[:], 0.0))
            masked(ident[:], [[-1, 128]], 0, 1, ALU.not_equal, 1.0)
            L(gp.memset(epsb[:], RMS_EPS))
            L(gp.memset(ones[:], 1.0))
            L(gp.memset(tri[:], 1.0))
            masked(tri[:], [[C, NCC], [1, C]], 0, -1)
            masked(tri[:], [[-C, NCC], [0, C]], 0, 1)
            L(gp.memset(same[:], 1.0))
            masked(same[:], [[-C, NCC], [0, C]], 0, 1)
            masked(same[:], [[C, NCC], [0, C]], C - 1, -1)
            for m, base in ((causal, 0), (strict, -1)):
                L(gp.memset(m[:], 1.0))
                for c in range(NCC):
                    masked(m[C * c:C * c + C], [[1, C]], base, -1)
            L(gp.memset(keep[:], 1.0))
            L(gp.memset(keep[:].rearrange("p (c t) -> p c t", t=C)[:, :, 0:1], 0.0))
            L(gp.memset(tok_rows, 0.0))
            gp.dma_start(tok_dram.rearrange("(b r) o -> b (r o)", r=CAP), tok_rows).then_inc(sg["tok_zeroed"], 16)
            pool.wait_ge(sg["tok_zeroed"], 16)
            gp.sem_inc(sg["consts"], 1)
            L(gp.memset(wide[0:CAP, 0, 0:D], 0.0))
            gp.dma_start(y_dram[NE * CAP:NBT * CAP, :].rearrange("(b r) d -> r b d", r=CAP),
                         wide[0:CAP, 0:1, 0:D].to_broadcast([CAP, NBT - NE, D])).then_inc(sg["y_zeroed"], 16)
            pool.wait_ge(sg["x_turned"], NI)
            L(gp.memset(pairX, 0.0))
            gp.affine_select(out=pairX, in_=pairX, compare_op=ALU.not_equal, fill=1.0, base=0,
                             pattern=[[1, C], [-1, C]], channel_multiplier=0).then_inc(sg["pairX_one"], 1)
            st4 = states[:].rearrange("p (b h) v -> p b h v", h=H)
            pool.wait_ge(sg["stA_in"], 16)
            pool.wait_ge(*mark["a_fg"])
            for b in range(NS):
                L(gp.tensor_tensor(st4[:, b], st4[:, b], smf[:, :, b:b + 1].to_broadcast([128, H, DV]), ALU.mult))
            gp.sem_inc(sg["stA_decayed"], 1)
            pool.wait_ge(sg["bank_free"], 4 + NEARLY + 4)
            pool.wait_ge(sg["n_sig"], 1)
            flat4 = lambda g: proj[:, g:g + H, :].rearrange("p h t -> p (h t)")
            gp.tensor_tensor(flat4(G_), flat4(G_), flat4(F_), ALU.mult).then_inc(sg["silu_done"], 1)
            pool.wait_ge(sg["stB_in"], 16)
            pool.wait_ge(sg["G_exps"], 2)
            for b in range(NS):
                L(gp.tensor_tensor(st4[:, b], st4[:, b], sbeg[:, :, b:b + 1].to_broadcast([128, H, DV]), ALU.mult))
            gp.sem_inc(sg["stB_decayed"], 1)
            pool.wait_ge(sg["bank_free"], 4 + NFT)
            pool.wait_ge(sg["n_sig"], 2)
            gp.tensor_tensor(flat4(Z_), flat4(Z_), flat4(F_), ALU.mult).then_inc(sg["silu_done"], 1)
            pool.wait_ge(sg["prompt_stored"], 32)
            pool.wait_ge(sg["oab_done"], KT)
            pool.wait_ge(sg["merged_ready"], KT)
            iot = lambda out, pattern, base, mult: L(gp.iota(out, pattern=pattern, base=base, channel_multiplier=mult,
                                                             allow_small_or_imprecise_dtypes=True))
            iot(iota_e, [[1, NE]], 0, 0)
            iot(iota_b, [[1, NBT]], 0, 0)
            iot(iota_p, [[0, 1]], 0, 1)
            iot(tokid, [[TP, NI]], 0, 1)
            iot(dump, [[LEAD - NS, TOP_K]], NBX * CAP, 1)
            L(gp.memset(triT, 1.0))
            masked(triT, [[1, TP]], -1, -1)
            L(gp.memset(hole, 1.0))
            masked(hole, [[0, 1]], -NS, 1)
            masked(hole, [[0, 1]], LEAD - 1, -1)
            L(gp.memset(lower, -1.0))
            for q in range(2):
                masked(lower[:, q:q + 1], [[0, 1]], -NE * (q + 1), 1)
            gp.sem_inc(sg["route_consts"], 1)
            pool.wait_ge(*mark["slot_ready"])
            for i in range(NI):
                for j in range(TOP_K):
                    gp.indirect_dma_start(tok_dram, bass.IndirectOffsetOnAxis(ap=slotw[:, i, j:j + 1], axis=0),
                                          tokid[:, i:i + 1], None).then_inc(sg["tok_scattered"], 16)
            pool.wait_ge(sg["tok_scattered"], 16 * NI * TOP_K)
            gp.dma_start(tok_rows, tok_dram.rearrange("(b r) o -> b (r o)", r=CAP)).then_inc(sg["tok_back"], 16)
            pool.wait_ge(*mark["nb_ready"])
            nb = pool.value_load(nbi[0:1, 0:1], min_val=NE, max_val=NBX)
            pool.wait_ge(*mark["tokT_ready"])
            pool.wait_ge(sg["xn_stored"], 16 * NI)

            def gather():
                gp.indirect_dma_start(xg, None, xn_dram, bass.IndirectOffsetOnAxis(ap=tkc, axis=0)) \
                    .then_inc(sg["xg_in"], 16)

            gp.tensor_copy(tkc, tokT[:, 0:1]).then_inc(sg["idx_ready"], 1)
            pool.wait_ge(sg["idx_ready"], 1)
            gather()
            with pool.Fori(1, nb + 1) as b:
                pool.wait_ge(sg["xg_in"], 16 * b)
                pool.wait_ge(sg["xg_turned"], b)
                pool.wait_ge(*mark["tokT_ready"])
                gp.tensor_copy(tkc, tokT[:, bass.ds(b, 1)]).then_inc(sg["idx_ready"], 1)
                pool.wait_ge(sg["idx_ready"], b + 1)
                pool.sem_inc(sg["wait_passed"], 1)
                gather()
            pool.wait_ge(sg["down_used"], DOWN0 + 4 * nb)
            pool.wait_ge(sg["y_stored"], 32 * nb + 32)
            pool.wait_ge(sg["y_zeroed"], 16)
            pool.sem_inc(sg["wait_passed"], 1)
            for i in range(NI):
                for j in range(TOP_K):
                    gp.indirect_dma_start(y_rows[i][j], None, y_dram,
                                          bass.IndirectOffsetOnAxis(ap=sloti[:, i, j:j + 1], axis=0)) \
                        .then_inc(sg[f"yg_in{i}"], 16)

        @block.tensor
        def _(pe):
            mm = nc.tensor.matmul
            tr = nc.tensor.transpose
            pe.wait_ge(sg["consts"], 1)
            pe.wait_ge(sg["prm_in"], 80)
            pe.wait_ge(sg["buf_in"], 16)
            tr(bank(0)[:, 0:66], prm_rows[0:66, :], ident[0:66, 0:66])
            for f in range(FC):
                last = tr(bank(1)[:, 24 * f:24 * f + 24], buf_rows[:, 128 * f:128 * f + 128], ident[0:24, 0:24])
            last.then_inc(mark["prm_turned"][0], 1)
            for i in range(NI):
                pe.wait_ge(sg["x_normed"], i + 1)
                for k in range(KT):
                    last = tr(bank(2 + 2 * i + k // 4)[:, TP * (k % 4):TP * (k % 4) + TP], xh[:, i, 128 * k:128 * k + 128],
                              ident[0:TP, 0:TP])
                last.then_inc(sg["x_turned"], 1)
            pe.wait_ge(sg["feat_ready"], 2 * NI)
            pe.wait_ge(*mark["prm_ready"])
            pe.wait_ge(sg["ab_in"], 16)
            for i in range(NI):
                for k in range(KT):
                    last = mm(bank(0)[0:TP, 8 * i:8 * i + 8], feat[:, k, TP * i:TP * i + TP], w_ab[:, k, :],
                              start=k == 0, stop=k == KT - 1)
            last.then_inc(mark["ab_done"][0], 1)
            with pe.Fori(0, NEARLY // (4 * NRING)) as it:
                for j in range(NRING):
                    pe.wait_ge(sg[f"win_in{j}"], 16 * (it + 1))
                    for m in range(4):
                        pe.wait_ge(sg["bank_free"], 12 * it + (4 * j + m) + 1)
                        for k in range(KT):
                            last = mm(bank(4 + m)[:, 0:T], win_buf[j][:, k, 128 * m:128 * m + 128], feat[:, k, :],
                                      start=k == 0, stop=k == KT - 1)
                        last.then_inc(sg["ptile_done"], 1)

            def project(n0, n1):
                for n in range(n0, n1):
                    if n % 4 == 0:
                        pe.wait_ge(sg[f"win_in{n // 4 % NRING}"], 16 * (n // 4 // NRING + 1))
                    pe.wait_ge(sg["bank_free"], 4 + n - 1)
                    for k in range(KT):
                        last = mm(bank(6 + n % 2)[:, 0:T], win_buf[n // 4 % NRING][:, k, 128 * (n % 4):128 * (n % 4) + 128],
                                  feat[:, k, :], start=k == 0, stop=k == KT - 1)
                    last.then_inc(sg["ptile_done"], 1)

            project(24, 26)
            pe.wait_ge(*mark["ab_taken"])
            pe.wait_ge(sg["bank_free"], 4 + NEARLY)
            for i in range(NI):
                for h in range(H):
                    last = tr(bank(i)[0:TP, 128 * h:128 * h + 128], proj[:, I_ + h, TP * i:TP * i + TP], ident[:])
                last.then_inc(sg["vA_turned"], 1)
            pe.wait_ge(*mark["g_ready"])
            mm(bank(3)[0:TP, 0:12], tri[:].rearrange("p a b -> p (a b)"), gt.rearrange("p i h -> p (i h)"))
            mm(bank(3)[0:TP, 16:28], same[:].rearrange("p a b -> p (a b)"), gt.rearrange("p i h -> p (i h)")) \
                .then_inc(mark["cum_done"][0], 1)
            project(26, 28)
            pe.wait_ge(*mark["G_taken"])
            for g in range(2):
                pe.wait_ge(sg["sq_ready"], g + 1)
                if g:
                    pe.wait_ge(sg["vA_taken"], NI + 1)
                at0 = 512 * 3 * (1 - g)
                for n in range(0, HT, 512):
                    e = min(n + 512, HT)
                    last = mm(psf[:, at0 + n:at0 + e], ones[:], cv[g][:, n:e], start=True, stop=True)
                last.then_inc(sg["l2_done"], 1)
            pe.wait_ge(sg["l2_root"], 2)

            def over_partitions(b0, src):
                for h in range(H):
                    for i in range(NI):
                        last = mm(bank(b0 + i)[:, TP * h:TP * h + TP], src[:, i, h:h + 1].to_broadcast([TP, 128]),
                                  tri[:].rearrange("p a b -> p (a b)") if b0 == 0 else ident[0:TP, 0:TP], start=True, stop=True)
                    if b0 == 0:
                        last = mm(bank(0)[:, H * TP + NS * h:H * TP + NS * h + NS], src[:, 0, h:h + 1].to_broadcast([TP, 128]),
                                  ident[0:TP, 0:NS], start=True, stop=True)
                return last

            over_partitions(0, gt).then_inc(mark["bcast_done"][0], 1)
            pe.wait_ge(*mark["conv_packed"])
            for f in range(FC):
                last = tr(bank(3 + f // 4)[0:NS + 3, 128 * (f % 4):128 * (f % 4) + 128], conv_pack[:, f, :], ident[:])
            last.then_inc(mark["conv_turned"][0], 1)
            project(28, 30)
            pe.wait_ge(sg["scA_ops"], 2)
            pe.wait_ge(sg["conv_rows"], 1)
            for i in range(NI):
                for c in range(NCC):
                    col = TP * i + C * c
                    for h in range(H):
                        last = mm(bank(3)[C * c:C * c + C, C * (H * i + h):C * (H * i + h) + C], proj[:, F_ + h, col:col + C],
                                  wideh(0)[:, h, col:col + C], start=True, stop=True)
            last.then_inc(mark["scA_done"][0], 1)
            project(30, 31)
            pe.wait_ge(sg["G_diffs"], NCC)
            pe.wait_ge(sg["G_exps"], 2)
            pe.wait_ge(sg["b_normed"], 2)
            qk = proj[:, QB_:KB_ + H, :].rearrange("p (a h) t -> p h a t", a=2)
            for i in range(NI):
                for c in range(NCC):
                    col = TP * i + C * c
                    for h in range(H):
                        n = H * i + h
                        last = mm(bank(n // 8)[C * c:C * c + C, 64 * (n % 8):64 * (n % 8) + 64],
                                  proj[:, KB_ + h, col:col + C], qk[:, h, :, col:col + C], start=True, stop=True)
            last.then_inc(mark["scB_done"][0], 1)
            pe.wait_ge(*mark["kA_ready"])
            for i in range(NI):
                if i == 2:
                    pe.wait_ge(*mark["PT_ready"])
                for h in range(H):
                    last = tr(bank((4, 5, 3)[i])[0:TP, 128 * h:128 * h + 128], proj[:, Q_ + h, TP * i:TP * i + TP], ident[:])
                last.then_inc(sg["kA_turned"], 1)
            pe.wait_ge(sg["kA_taken"], NI)
            over_partitions(3, bt).then_inc(mark["beta_done"][0], 1)
            project(31, 33)
            pe.wait_ge(*mark["MT_ready"])
            tb = (2, 3, 4, 5, 0, 1)
            for src, at0, name in ((KB_, 0, "kB_turned"), (VB_, NI, "vB_turned")):
                for i in range(NI):
                    for h in range(H):
                        last = tr(bank(tb[at0 + i])[0:TP, 128 * h:128 * h + 128], proj[:, src + h, TP * i:TP * i + TP], ident[:])
                    last.then_inc(sg[name], 1)

            def spread(name, b, base, banks):
                if base + b >= 2:
                    pe.wait_ge(sg["spread_used"], base + b - 1)
                mm(bank(banks[b % 2])[:, :], ident[64:64 + NS, 64 + b:65 + b].to_broadcast([NS, 128]), v_row,
                   start=True, stop=True).then_inc(sg[name], 1)

            def stepA(n):
                i, c = n // NCC, n % NCC
                col, rows = TP * i + C * c, slice(C * c, C * c + C)
                first = n == 0
                for h in range(H):
                    mm(bank(n % 2)[:, 128 * h:128 * h + 128], kdA[rows, i, h, :], vtA[rows, i, h, :], start=True, stop=True)
                if n:
                    pe.wait_ge(sg["stateA_upd"], H * n)
                if n >= 2:
                    pe.wait_ge(sg["oA_taken"], n - 1)
                for h in range(H):
                    o = bank(5 - n % 2)[:, C * h:C * h + C]
                    last = mm(o, vtA[rows, i, h, :], PT[rows, i, h, :], start=True, stop=first)
                    if not first:
                        last = mm(o, spA[:, h, :], proj[:, I_ + h, col:col + C], start=False, stop=True)
                last.then_inc(sg["stepA_done"], 1)

            pe.wait_ge(sg["kB_taken"], 2)
            spread("stA_spread", 0, 0, (2, 3))
            spread("stA_spread", 1, 0, (2, 3))
            pe.wait_ge(sg["vB_taken"], NI)
            stepA(0)
            for b in range(2, NS):
                spread("stA_spread", b, 0, (2, 3))
            pe.wait_ge(sg["stA_new"], NS * H)
            for b in range(NS):
                for h in range(H):
                    last = mm(bank(2)[:, NS * h + b:NS * h + b + 1], states[:, H * b + h, :], smq[:, h, b:b + 1],
                              start=True, stop=True)
            last.then_inc(mark["stA_read"][0], 1)
            for n in range(1, NI * NCC):
                stepA(n)
                project(FILL[n - 1], FILL[n])
            pe.wait_ge(sg["oA_sample"], 1)
            pe.wait_ge(sg["spread_used"], NS)
            pe.wait_ge(sg["n_sq"], 1)

            def square_sums(src):
                for n in range(0, HT, 512):
                    e = min(n + 512, HT)
                    last = mm(psf[:, 3 * 512 + n:3 * 512 + e], ones[:], src[:, n:e], start=True, stop=True)
                last.then_inc(sg["n_sum"], 1)

            square_sums(proj[:, I_:I_ + H, :].rearrange("p h t -> p (h t)"))

            def out_tile(b, w, g, m):
                for k in range(H):
                    last = mm(bank(b)[:, 0:T], w[:, k, 128 * m:128 * m + 128], proj[:, g + k, :], start=k == 0, stop=k == H - 1)
                return last

            pe.wait_ge(sg["stB_decayed"], 1)
            pe.wait_ge(sg["bank_free"], 4 + NFT)
            for b in range(NS):
                for h in range(H):
                    last = mm(bank(7)[:, NS * h + b:NS * h + b + 1], states[:, H * b + h, :], gmk[:, h, b:b + 1],
                              start=True, stop=True)
            last.then_inc(mark["stB_kS"][0], 1)
            pe.wait_ge(sg["stateA_upd"], H * NI * NCC)
            pe.wait_ge(sg["XT_in"], 16 * NCC)
            for h in range(H):
                for i in range(NI):
                    for c in range(NCC):
                        last = mm(bank(c)[:, C * (NI * h + i):C * (NI * h + i) + C], kbe[C * c:C * c + C, i, h, :],
                                  XT[C * c:C * c + C, i, h, :], start=True, stop=True)
            last.then_inc(mark["wT_done"][0], 1)
            pe.wait_ge(*mark["stB_delta"])
            pe.wait_ge(sg["n_root"], 1)
            for h in range(H):
                last = tr(bank(3)[0:NS, 128 * h:128 * h + 128], sdelta[:, h, :], ident[:])
            last.then_inc(mark["stB_turned"][0], 1)

            def stepB_start(n):
                i, c = n // NCC, n % NCC
                rows = slice(C * c, C * c + C)
                for h in range(H):
                    last = mm(bank(6)[rows, 128 * h:128 * h + 128], XT[rows, i, h, :], vb[rows, i, h, :],
                              start=h == 0, stop=n == 0 and h == H - 1)
                return last

            pe.wait_ge(sg["bank_free"], 4 + NFT)
            stepB_start(0).then_inc(sg["vnew_done"], 1)
            pe.wait_ge(sg["wT_taken"], 1)
            pe.wait_ge(*mark["qdec_ready"])
            for n in range(NI * NCC):
                i, c = n // NCC, n % NCC
                col, rows = TP * i + C * c, slice(C * c, C * c + C)
                if n:
                    pe.wait_ge(sg["stateB_upd"], H * n)
                    for h in range(H):
                        last = mm(bank(6)[rows, 128 * h:128 * h + 128], wideh(1)[:, h, col:col + C], spB[:, h, :],
                                  start=False, stop=h == H - 1)
                    last.then_inc(sg["vnew_done"], 1)
                if n >= 2:
                    pe.wait_ge(sg["oB_taken"], n - 1)
                o = [bank(7 * (n % 2))[:, C * h:C * h + C] for h in range(H)]
                if n:
                    for h in range(H):
                        mm(o[h], spB[:, h, :], proj[:, QB_ + h, col:col + C], start=h == 0, stop=False)
                pe.wait_ge(sg["vnew_taken"], n + 1)
                for h in range(H):
                    last = mm(bank(1 + n % 2)[:, 128 * h:128 * h + 128], kdB[rows, i, h, :],
                              v_new[rows, 128 * h:128 * h + 128], start=True, stop=True)
                last.then_inc(sg["kvB_done"], 1)
                for h in range(H):
                    last = mm(o[h], v_new[rows, 128 * h:128 * h + 128], AT[rows, i, h, :], start=n == 0 and h == 0,
                              stop=h == H - 1)
                last.then_inc(sg["oB_done"], 1)
                if n + 1 < NI * NCC:
                    stepB_start(n + 1)
                if n == 0:
                    pe.wait_ge(sg["stB_row"], 1)
                if n < NS:
                    pe.wait_ge(sg["spread_used"], NS + n)
                    spread("stB_spread", n, NS, (3, 3))
                if n:
                    b = n - 1
                    pe.wait_ge(sg["stB_new"], n * H)
                    for h in range(H):
                        last = mm(bank(4)[:, NS * h + b:NS * h + b + 1], states[:, H * b + h, :], gmq[:, h, b:b + 1],
                                  start=True, stop=True)
                    if n == NS:
                        last.then_inc(mark["stB_read"][0], 1)
                    pe.wait_ge(sg["ya_ready"], 1)
                    pe.wait_ge(sg["woa_in"], 16)
                    if b:
                        pe.wait_ge(sg["oa_gated"], b)
                    out_tile(5, woa_sb, G_, b).then_inc(sg["oa_done"], 1)

            pe.wait_ge(sg["oB_sample"], 1)
            pe.wait_ge(sg["n_sq"], 2)
            pe.wait_ge(sg["oa_gated"], KT)
            pe.wait_ge(sg["stB_new"], NS * H)
            square_sums(wide[:, 1, :])
            pe.wait_ge(sg["n_root"], 2)
            pe.wait_ge(sg["stateB_upd"], H * NI * NCC)
            pe.wait_ge(sg["ya_ready"], 2)
            pe.wait_ge(sg["wob_in"], 16)
            for m in range(KT):
                out_tile(m, wob_sb, Z_, m).then_inc(sg["oab_done"], 1)
            pe.wait_ge(sg["merged_ready"], KT)
            pe.wait_ge(sg["wout_in"], 16)
            pe.wait_ge(sg["wout2_in"], 16)
            for i in range(NI):
                for j in range(2):
                    for k in range(KT):
                        w = wout_lo[:, k, :] if k < 4 else wout_hi[:, k - 4, :]
                        last = mm(bank(2 * i + j)[0:TP, :], feat[:, k, TP * i:TP * i + TP], w[:, 512 * j:512 * j + 512],
                                  start=k == 0, stop=k == KT - 1)
                    last.then_inc(sg["mix_done"], 1)
            for i in range(NI):
                pe.wait_ge(sg["x2_normed"], i + 1)
                if i == 1:
                    pe.wait_ge(sg["x2_ready"], 2 * NI)
                for k in range(KT):
                    last = tr(bank((6 + 2 * i) % 8 + k // 4)[:, TP * (k % 4):TP * (k % 4) + TP],
                              x2h[:, i, 128 * k:128 * k + 128], ident[0:TP, 0:TP])
                last.then_inc(sg["x2_turned"], 1)
            pe.wait_ge(sg["route_in"], 32)
            pe.wait_ge(sg["xnT_ready"], 2 * NI)
            for i in range(NI):
                for k in range(KT):
                    last = mm(bank(4)[0:TP, NE * i:NE * i + NE], xnT[:, k, TP * i:TP * i + TP], w_rt[:, k, :],
                              start=k == 0, stop=k == KT - 1)
            last.then_inc(mark["logits_done"][0], 1)
            pe.wait_ge(*mark["sel_done"])
            pe.wait_ge(sg["route_consts"], 1)
            for i in range(NI):
                mm(bank(5)[0:TP, NE * i:NE * i + NE], triT, selm[:, i, :], start=True, stop=i == 0)
                for p in range(i):
                    mm(bank(5)[0:TP, NE * i:NE * i + NE], ones[0:TP, 0:TP], selm[:, p, :], start=False, stop=p == i - 1)
            for i in range(NI):
                last = mm(bank(6)[0:NE, 0:1], selm[:, i, :], ones[0:TP, 0:1], start=i == 0, stop=i == NI - 1)
            last.then_inc(mark["cnt_done"][0], 1)
            pe.wait_ge(*mark["ext_ready"])
            mm(bank(6)[0:NE, 8:9], strict[0:NE, 0:NE], extc[:, 0:1], start=True, stop=True)
            mm(bank(6)[0:1, 16:17], extc[:, 0:1], ones[0:NE, 0:1], start=True, stop=True)
            mm(bank(6)[0:TP, 64:64 + NE], extc[:, 0:1].to_broadcast([NE, TP]), strict[0:NE, 0:NE], start=True, stop=True) \
                .then_inc(mark["off_done"][0], 1)
            pe.wait_ge(*mark["eh_ready"])
            mm(bank(6)[0:1, 128:128 + NBT], iota_p, eh, start=True, stop=True).then_inc(mark["blk_done"][0], 1)
            pe.wait_ge(sg["tok_back"], 16)
            tr(bank(7)[0:CAP, 0:NBT], tok_rows, ident[0:NBT, 0:NBT]).then_inc(mark["tok_turned"][0], 1)

            pe.wait_ge(*mark["nb_ready"])
            nb = pe.value_load(nbi[0:1, 0:1], min_val=NE, max_val=NBX)
            rows_T = bank(2).rearrange("p (k t) -> p k t", k=KT)
            hid_T = bank(3).rearrange("p (c t) -> p c t", c=4)
            pe.wait_ge(*mark["tokT_ready"])
            pe.wait_ge(sg["b3_ready"], 3)

            def turn_rows(b):
                pe.wait_ge(sg["xg_in"], 16 * (b + 1))
                pe.sem_inc(sg["wait_passed"], 1)
                for k in range(KT):
                    last = tr(rows_T[:, k, :], xg[:, 128 * k:128 * k + 128], ident[0:CAP, 0:CAP])
                last.then_inc(sg["xg_turned"], 1)

            def gate_up(b):
                pe.wait_ge(sg["xg_ready"], b + 1)
                pe.wait_ge(sg["sel_gu_ready"], b + 1)
                pe.wait_ge(sg["up_clipped"], b + 1)
                for j in range(4):
                    mm(bank(j // 2)[64 * (j % 2):64 * (j % 2) + 64, :], sel_gu, b3[:, 512 * j:512 * j + 512],
                       start=True, stop=False)
                for k in range(KT):
                    pe.wait_ge(w_arrived[k], 16 * (b + 1))
                    for j in range(4):
                        last = mm(bank(j // 2)[64 * (j % 2):64 * (j % 2) + 64, :], xgT[:, k, :],
                                  ring[:, k, 512 * j:512 * j + 512], start=False, stop=k == KT - 1)
                    last.then_inc(sg["gu_used"], 1)

            def down(b):
                pe.wait_ge(sg["hid_ready"], b + 1)
                pe.sem_inc(sg["wait_passed"], 1)
                for c in range(4):
                    last = tr(hid_T[:, c, :], hid[:, 128 * c:128 * c + 128], ident[:])
                last.then_inc(sg["hid_turned"], 1)
                pe.wait_ge(sg["sel_dn_ready"], b + 1)
                pe.wait_ge(sg["y_ready"], b + 1)
                for j in range(2):
                    mm(bank(4)[64 * j:64 * j + 64, :], sel_dn, b3[:, 2048 + 512 * j:2560 + 512 * j], start=True, stop=False)
                pe.wait_ge(sg["hidT_ready"], b + 1)
                for k in range(KT):
                    if k % 2 == 0:
                        pe.wait_ge(w_arrived[KT + k // 2], 16 * (b + 1))
                    for j in range(2):
                        n = (k % 2) * 1024 + 512 * j
                        last = mm(bank(4)[64 * j:64 * j + 64, :], hidT[:, k % 4, 64 * (k // 4):64 * (k // 4) + 64],
                                  ring[:, KT + k // 2, n:n + 512], start=False, stop=k == KT - 1)
                    if k % 2:
                        last.then_inc(sg["down_used"], 1)

            pe.sem_inc(sg["down_used"], DOWN0)
            turn_rows(0)
            gate_up(0)
            turn_rows(1)
            with pe.Fori(0, nb - 1) as b:
                gate_up(b + 1)
                turn_rows(b + 2)
                down(b)
            down(nb - 1)

        @block.scalar
        def _(act):
            L = Steps(act, "act_step")
            f = nc.scalar.activation
            act.dma_start(alb, a_log.to_broadcast([TP, H])).then_inc(sg["par_in"], 16)
            act.dma_start(dtb, dt_bias.to_broadcast([TP, H])).then_inc(sg["par_in"], 16)
            act.dma_start(states[:], state_hgrn[0].rearrange("b h k v -> k (b h) v")).then_inc(sg["stA_in"], 16)
            act.dma_start(w_rt[:], w_router[0].rearrange("(k p) n -> p k n", p=128)).then_inc(sg["route_in"], 16)
            act.dma_start(conv_sample[0, :, 0:CW - 2, :], state_conv[0, :, 1:CW - 1, :]).then_inc(sg["conv_stored"], 16)
            for i, n in enumerate((48, 16, 16)):
                act.wait_ge(sg[f"x_in{i}"], n)
                L(f(xh[:, i, :], x_tok[:, i, :], ACT.Square, accum_out=ss[:, i:i + 1]))
            act.wait_ge(sg["consts"], 1)
            L.tell(f(rstd, ss, ACT.Sqrt, scale=1.0 / D, bias=epsb[0:TP, 0:1]), "x_summed")
            act.wait_ge(sg["par_in"], 32)
            L(f(alb, alb, ACT.Exp))
            act.wait_ge(*mark["lb_diff"])
            L(f(lbt, lbt, ACT.Exp))
            L.tell(f(omlb, omlb, ACT.Exp), "lb_exp")
            act.wait_ge(*mark["g_pre"])
            L(f(Gl, Gl, ACT.Exp))
            L.tell(f(Gl, Gl, ACT.Ln, bias=1.0), "g_exp")
            L.tell(f(bt, ab[:, :, H:2 * H], ACT.Sigmoid), "beta_sig")
            group = lambda g: proj[:, g:g + H, :]
            cvh = lambda g: cv[g].rearrange("p (h t) -> p h t", h=H)

            def conv_sigmoid(g):
                act.wait_ge(sg["conv_out"], g + 1)
                L.tell(f(group(QB_ + H * g), cvh(g), ACT.Sigmoid), "conv_sig", g + 1)

            def inverse_root(out, src, done, n, scale=1.0):
                L(f(out, src, ACT.Ln, scale=scale, bias=epsb[:, 0:1]))
                L.tell(f(out, out, ACT.Exp, scale=-0.5), done, n)

            def take_tiles(n0, n1):
                for n in range(n0, n1):
                    act.wait_ge(sg["ptile_done"], n + 1)
                    f(proj[:, 4 * ORDER[n // 4] + n % 4, :], bank(4 + n % 4 if n < NEARLY else 6 + n % 2)[:, 0:T], ACT.Copy) \
                        .then_inc(sg["bank_free"], 1)

            with act.Fori(0, FC // 4) as it:
                for m in range(4):
                    act.wait_ge(sg["ptile_done"], 4 * it + m + 1)
                    f(proj[:, bass.ds(4 * it + (QB_ + m), 1), :], bank(4 + m)[:, 0:T].rearrange("p (a t) -> p a t", a=1),
                      ACT.Copy).then_inc(sg["bank_free"], 1)
            act.wait_ge(sg["y_zeroed"], 16)
            take_tiles(12, 16)
            conv_sigmoid(0)
            act.wait_ge(sg["bank_free"], 4 + 16)
            L.tell(f(wideh(0), group(Q_), ACT.Sigmoid), "a_sig", 1)
            take_tiles(16, 20)
            conv_sigmoid(1)
            act.wait_ge(sg["bank_free"], 4 + 20)
            L.tell(f(wideh(1), group(F_), ACT.Sigmoid), "a_sig", 2)
            L.tell(f(wideh(2), group(F_), ACT.Sigmoid, scale=-1.0), "a_sig", 3)
            take_tiles(20, 24)
            conv_sigmoid(2)
            for g in range(2):
                act.wait_ge(sg["conv_done"], g + 1)
                L.tell(f(cvh(g), group(QB_ + H * g), ACT.Square), "sq_ready", g + 1)
            take_tiles(24, 26)
            heads = lambda b: bank(b)[0:TP, :].rearrange("p (h n) -> p h n", h=H)
            for i in range(NI):
                act.wait_ge(sg["vA_turned"], i + 1)
                if i == 0:
                    act.wait_ge(sg["x_turned"], NI)
                L.tell(f(vtA[:, i], heads(i), ACT.Copy), "vA_taken", i + 1)
            L.tell(f(v_row, bank(0)[0:NS, :], ACT.Copy), "vA_taken", NI + 1)
            act.wait_ge(*mark["a_fg"])
            L.tell(f(group(F_), wideh(1), ACT.Ln), "a_ln")
            take_tiles(26, 28)
            act.wait_ge(sg["l2_done"], 1)
            inverse_root(cv[0], psf[:, 1536:1536 + HT], "l2_root", 1)
            act.wait_ge(sg["l2_done"], 2)
            inverse_root(cv[1], psf[:, 0:HT], "l2_root", 2)
            act.wait_ge(*mark["a_diff"])
            L.tell(f(wideh(0), group(F_), ACT.Exp), "a_exp", 1)
            L.tell(f(group(F_), group(F_), ACT.Exp, scale=-1.0), "a_exp", 2)
            act.wait_ge(sg["vA_turned"], NI)
            L.tell(f(group(I_), wideh(1), ACT.Exp), "a_expb")
            act.wait_ge(*mark["bcast_done"])
            act.wait_ge(sg["conv_done"], 3)
            L.tell(f(cv[2].rearrange("p (h i t) -> p i h t", h=H, i=NI),
                     ps[:, 0:NI, 0:H * TP].rearrange("p i (h t) -> p i h t", h=H), ACT.Exp), "G_exps", 1)
            L.tell(f(sbeg, bank(0)[:, H * TP:H * TP + H * NS].rearrange("p (h b) -> p h b", h=H), ACT.Exp), "G_exps", 2)
            act.wait_ge(*mark["conv_turned"])
            L.tell(f(conv_new, psf[0:NS + 3, 1536:1536 + DC], ACT.Copy), "conv_rows")
            act.dma_start(conv_sample[0, :, CW - 2, :], conv_new[0:NS, :]).then_inc(sg["conv_stored"], 16)
            act.dma_start(conv_prompt[0, 0], conv_new[NS:NS + 3, :]).then_inc(sg["conv_stored"], 16)
            take_tiles(28, 30)
            act.wait_ge(*mark["lt_diff"])
            L.tell(f(LT, LT, ACT.Exp), "lt_exp", 1)
            L.tell(f(bG, Gt, ACT.Exp), "lt_exp", 2)
            L.tell(f(eGl, eGl, ACT.Exp), "lt_exp", 3)
            act.wait_ge(*mark["a_kdiff"])
            L.tell(f(group(Q_), group(Q_), ACT.Exp), "a_kexp")
            take_tiles(30, 31)
            for i in range(NI):
                act.wait_ge(sg["kA_turned"], i + 1)
                L.tell(f(kdA[:, i], heads((4, 5, 3)[i]), ACT.Copy), "kA_taken", i + 1)
            take_tiles(31, 33)
            act.wait_ge(*mark["scA_done"])
            act.wait_ge(sg["bank_free"], 4 + NEARLY + 4)
            L.tell(f(group(F_), group(G_), ACT.Sigmoid), "n_sig", 1)
            def takeA(n):
                col = TP * (n // NCC) + C * (n % NCC)
                act.wait_ge(sg["stepA_done"], n + 1)
                L.tell(f(proj[:, Q_:Q_ + H, col:col + C], bank(5 - n % 2)[:, 0:H * C]
                         .rearrange("p (h t) -> p h t", h=H), ACT.Copy), "oA_taken", n + 1)

            takeA(0)
            act.wait_ge(*mark["stA_read"])
            L.tell(f(soA, bank(2)[:, 0:H * NS].rearrange("p (h b) -> p h b", h=H), ACT.Copy), "oA_sample")
            L(f(proj[:, Q_:Q_ + H, 0:NS], soA, ACT.Copy))
            for n in range(1, NI * NCC):
                takeA(n)
                take_tiles(FILL[n - 1], FILL[n])
            L.tell(f(group(I_), group(Q_), ACT.Square), "n_sq", 1)
            act.wait_ge(sg["n_sum"], 1)
            inverse_root(group(I_).rearrange("p h t -> p (h t)"), psf[:, 1536:1536 + HT], "n_root", 1, 1.0 / DV)
            act.wait_ge(sg["silu_done"], 1)
            act.wait_ge(sg["bank_free"], 4 + NFT)
            L.tell(f(proj[:, GA_:GB_, :], proj[:, GA_:GB_, :], ACT.Sigmoid), "gates_sig", 1)
            L.tell(f(group(F_), group(Z_), ACT.Sigmoid), "n_sig", 2)
            L.tell(f(proj[:, GB_:NFT, :], proj[:, GB_:NFT, :], ACT.Sigmoid), "gates_sig", 2)
            act.wait_ge(*mark["wT_done"])
            L.tell(f(W1.rearrange("p (n c t) -> p c n t", c=NCC, t=C),
                     ps[:, 0:NCC, 0:H * NI * C].rearrange("p c (n t) -> p c n t", t=C), ACT.Copy, scale=-1.0), "wT_taken")
            act.wait_ge(*mark["stB_turned"])
            L.tell(f(v_row, bank(3)[0:NS, :], ACT.Copy), "stB_row")

            def takeB(n):
                col = TP * (n // NCC) + C * (n % NCC)
                act.wait_ge(sg["oB_done"], n + 1)
                L.tell(f(proj[:, KB_:KB_ + H, col:col + C], bank(7 * (n % 2))[:, 0:H * C]
                         .rearrange("p (h t) -> p h t", h=H), ACT.Copy), "oB_taken", n + 1)

            for n in range(NI * NCC):
                rows = slice(C * (n % NCC), C * (n % NCC) + C)
                act.wait_ge(sg["vnew_done"], n + 1)
                L.tell(f(v_new[rows, :], bank(6)[rows, :], ACT.Copy), "vnew_taken", n + 1)
                takeB(n)
            act.wait_ge(*mark["stB_read"])
            L.tell(f(soB, bank(4)[:, 0:H * NS].rearrange("p (h b) -> p h b", h=H), ACT.Copy), "oB_sample")
            act.dma_start(gdn_sample[0].rearrange("b h k v -> k (b h) v"), states[:]).then_inc(sg["stB_stored"], 16)
            L(f(proj[:, KB_:KB_ + H, 0:NS], soB, ACT.Copy))
            L.tell(f(wideh(1), group(KB_), ACT.Square), "n_sq", 2)
            act.wait_ge(sg["n_sum"], 2)
            inverse_root(W1, psf[:, 1536:1536 + HT], "n_root", 2, 1.0 / DV)
            act.wait_ge(sg["ya_ready"], 2)
            for p in range(3):
                act.dma_start(b_f32[NE * p:NE * p + NE, 0:2 * D], b_gu[0]).then_inc(sg["bias_in"], 16)
                act.dma_start(b_f32[NE * p:NE * p + NE, 2 * D:3 * D], b_down[0]).then_inc(sg["bias_in"], 16)
            act.dma_start(br_b, b_router.to_broadcast([TP, NE])).then_inc(sg["route_in"], 16)
            act.wait_ge(sg["merged_ready"], KT)
            act.dma_start(nffn_b, norm_ffn.to_broadcast([TP, D])).then_inc(sg["nffn_in"], 16)
            act.dma_start(nfin_b, norm_final.rearrange("(a d) -> a d", a=1).to_broadcast([TP, D])).then_inc(sg["nfin_in"], 16)
            act.wait_ge(sg["bias_in"], 96)
            act.wait_ge(sg["prompt_stored"], 32)
            for q in range(3):
                if q:
                    act.wait_ge(sg["b3_less"], q)
                L.tell(f(b3, b_f32, ACT.Copy), "b3_ready", q + 1)
            act.wait_ge(sg["mix_done"], 2 * NI)
            for i in range(NI):
                act.wait_ge(sg["x2_ready"], 2 * i + 2)
                L(f(x2h[:, i, :], x_tok[:, i, :], ACT.Square, accum_out=ss[:, i:i + 1]))
                L.tell(f(rstd[:, i:i + 1], ss[:, i:i + 1], ACT.Sqrt, scale=1.0 / D, bias=epsb[0:TP, 0:1]), "x2_summed", i + 1)
            for i in range(NI):
                act.wait_ge(sg["x2_normed"], i + 1)
                act.dma_start(xn_dram[TP * i:TP * i + TP, :], x2h[:, i, :]).then_inc(sg["xn_stored"], 16)
                act.wait_ge(sg["x2_turned"], i + 1)
                for j in range(2):
                    src = bank((6 + 2 * i) % 8 + j)[:, 0:4 * TP].rearrange("p (k t) -> p k t", k=4)
                    L.tell(f(xnT[:, 4 * j:4 * j + 4, TP * i:TP * i + TP], src, ACT.Copy), "xnT_ready", 2 * i + j + 1)
            act.wait_ge(*mark["cnt_done"])
            L.tell(f(gate, gate, ACT.Exp), "top_exp")
            act.wait_ge(*mark["nb_ready"])
            nb = act.value_load(nbi[0:1, 0:1], min_val=NE, max_val=NBX)
            act.wait_ge(*mark["eh_ready"])
            act.sem_inc(sg["y_stored"], 32)
            act.sem_inc(sg["y_ready"], 1)

            def pick(out, b, name):
                f(out, eh3[:, bass.ds(b, 1)].to_broadcast([3 * NE, CAP]), ACT.Copy).then_inc(sg[name], 1)

            pick(sel_gu, 0, "sel_gu_ready")
            with act.Fori(0, nb) as b:
                pick(sel_dn, b, "sel_dn_ready")
                act.wait_ge(sg["gate_clipped"], b + 1)
                pick(sel_gu, b + 1, "sel_gu_ready")
                f(hid_s, hid_g, ACT.Sigmoid, scale=SWIGLU_ALPHA).then_inc(sg["sig_ready"], 1)
                act.wait_ge(sg["hid_turned"], b + 1)
                f(hidT, bank(3).rearrange("p (c t) -> p c t", c=4), ACT.Copy).then_inc(sg["hidT_ready"], 1)
                act.wait_ge(sg["down_used"], DOWN0 + 4 * b + 4)
                act.wait_ge(sg["y_stored"], 32 * (b + 1))
                f(y_out, bank(4), ACT.Copy).then_inc(sg["y_ready"], 1)
                act.wait_ge(sg["y_ready"], b + 2)
                for j in range(2):
                    act.dma_start(y_dram[bass.ds(b * CAP, CAP), HF * j:HF * j + HF], y_out[64 * j:64 * j + 64, :]) \
                        .then_inc(sg["y_stored"], 16)
            for i in range(NI):
                act.wait_ge(sg["yg_summed"], i + 1)
                L(f(x2h[:, i, :], x_tok[:, i, :], ACT.Square, accum_out=ss[:, i:i + 1]))
                L.tell(f(rstd[:, i:i + 1], ss[:, i:i + 1], ACT.Sqrt, scale=1.0 / D, bias=epsb[0:TP, 0:1]), "f_summed", i + 1)
            for i in range(NI):
                act.wait_ge(sg["f_ready"], i + 1)
                if i == 0:
                    act.dma_start(y_sample[:, 0, :], x_tok[0:NS, 0, :]).then_inc(sg["out_stored"], 16)
                    act.dma_start(y_prompt[0, 0:TP - 32, :], x_tok[32:TP, 0, :]).then_inc(sg["out_stored"], 16)
                else:
                    act.dma_start(y_prompt[0, TP * i - 32:TP * i + 64, :], x_tok[:, i, :]).then_inc(sg["out_stored"], 16)
            act.wait_ge(sg["out_stored"], 16 * (NI + 1))
            act.wait_ge(sg["conv_stored"], 48)

        @block.vector
        def _(dve):
            L = Steps(dve, "dve_step")
            v = nc.vector
            tt, ts, stt = v.tensor_tensor, v.tensor_scalar, v.scalar_tensor_tensor
            group = lambda g: proj[:, g:g + H, :]
            flat = lambda g: proj[:, g:g + H, :].rearrange("p h t -> p (h t)")
            last_dim = lambda a: a.rearrange("p i (h o) -> p i h o", o=1)
            dve.wait_ge(*mark["prm_turned"])
            L(v.tensor_copy(prmT, bank(0)[:, 0:66]))
            L.tell(v.tensor_copy(bufT.rearrange("p f b j -> p (f b j)"), bank(1)[:, 0:288]), "prm_ready")
            L(tt(lbt, prmT[:, 8:12], prmT[:, 12:16], ALU.max))
            L(tt(omlb, prmT[:, 12:16], lbt, ALU.subtract))
            L.tell(tt(lbt, prmT[:, 8:12], lbt, ALU.subtract), "lb_diff")
            dve.wait_ge(sg["x_summed"], 1)
            L(v.reciprocal(rstd, rstd))
            for i in range(NI):
                L.tell(ts(xh[:, i, :], x_tok[:, i, :], rstd[:, i:i + 1], None, ALU.mult), "x_normed", i + 1)
            for i in range(NI):
                dve.wait_ge(sg["x_turned"], i + 1)
                for j in range(2):
                    src = bank(2 + 2 * i + j)[:, 0:4 * TP].rearrange("p (k t) -> p k t", k=4)
                    w = prmT[:, 4 * j:4 * j + 4].rearrange("p (k o) -> p k o", o=1).to_broadcast([128, 4, TP])
                    L.tell(tt(feat[:, 4 * j:4 * j + 4, TP * i:TP * i + TP], src, w, ALU.mult), "feat_ready", 2 * i + j + 1)
            dve.sem_inc(sg["bank_free"], 4)
            dve.wait_ge(sg["lb_exp"], 1)
            L(tt(smx[:, 0, 0:H], lbt, omlb, ALU.add))
            L(v.reciprocal(smx[:, 0, 0:H], smx[:, 0, 0:H]))
            L(tt(lbt, lbt, smx[:, 0, 0:H], ALU.mult))
            L(ts(omlb, lbt, -1.0, 1.0, ALU.mult, ALU.add))
            dve.wait_ge(*mark["ab_done"])
            L.tell(v.tensor_copy(ab, bank(0)[0:TP, 0:24].rearrange("p (i h) -> p i h", i=NI)), "ab_taken")
            dve.wait_ge(sg["par_in"], 32)
            dtb3 = dtb.rearrange("p (o h) -> p o h", o=1).to_broadcast([TP, NI, H])
            alb3 = alb.rearrange("p (o h) -> p o h", o=1).to_broadcast([TP, NI, H])
            L(tt(Gt, ab[:, :, 0:H], dtb3, ALU.add))
            L(ts(gt, Gt, 0.0, None, ALU.max))
            L(ts(Gl, Gt, -1.0, None, ALU.mult))
            L.tell(tt(Gl, Gt, Gl, ALU.min), "g_pre")
            dve.wait_ge(sg["g_exp"], 1)
            L(tt(gt, gt, Gl, ALU.add))
            L(tt(gt, gt, alb3, ALU.mult))
            L(ts(gt, gt, -1.0, None, ALU.mult))
            dve.wait_ge(sg["beta_sig"], 1)
            L(v.tensor_copy(btm, bt))
            L.tell(v.memset(btm[0:LEAD, 0, :], 0.0), "g_ready")
            dve.wait_ge(sg["bank_free"], 4 + FC)
            raw = proj[:, QB_:QB_ + FC, :]
            L(v.tensor_copy(conv_pack[:, :, 0:NS], raw[:, :, 0:NS]))
            L.tell(v.tensor_copy(conv_pack[:, :, NS:NS + 3], raw[:, :, T - 3:T]), "conv_packed")
            cw = lambda j: prmT[:, 16 + FC * j:16 + FC * j + FC].rearrange("p (f o) -> p f o", o=1).to_broadcast([128, FC, NS])
            L(tt(smx, conv_pack[:, :, 0:NS], cw(CW - 1), ALU.mult))
            for j in range(CW - 1):
                L(tt(smy, bufT[:, :, :, j], cw(j), ALU.mult))
                L(tt(smx, smx, smy, ALU.add))
            for g in range(3):
                cvg = cv[g].rearrange("p (h t) -> p h t", h=H)
                L(v.memset(cvg[:, :, NS:LEAD], 0.0))
                L(v.tensor_copy(cvg[:, :, 0:NS], smx[:, H * g:H * g + H, :]))
                for h in range(H):
                    fi = H * g + h
                    L(ts(cvg[:, h, LEAD:T], raw[:, fi, LEAD:T], prmT[:, 16 + FC * (CW - 1) + fi:17 + FC * (CW - 1) + fi],
                         None, ALU.mult))
                    for s in range(1, CW):
                        w = prmT[:, 16 + FC * (CW - 1 - s) + fi:17 + FC * (CW - 1 - s) + fi]
                        L(stt(out=cvg[:, h, LEAD + s:T], in0=raw[:, fi, LEAD:T - s], scalar=w, in1=cvg[:, h, LEAD + s:T],
                              op0=ALU.mult, op1=ALU.add))
                dve.sem_inc(sg["conv_out"], 1)
            for g in range(3):
                dve.wait_ge(sg["conv_sig"], g + 1)
                L.tell(tt(flat(QB_ + H * g), flat(QB_ + H * g), cv[g], ALU.mult), "conv_done", g + 1)
            dve.wait_ge(sg["a_sig"], 3)
            L(stt(out=flat(Q_), in0=flat(Q_), scalar=SCALE, in1=W0, op0=ALU.mult, op1=ALU.mult))
            for h in range(H):
                L(ts(wideh(1)[:, h, :], wideh(1)[:, h, :], omlb[:, h:h + 1], lbt[:, h:h + 1], ALU.mult, ALU.add))
            L(tt(wideh(2), wideh(2), omlb.rearrange("p (h o) -> p h o", o=1).to_broadcast([128, H, T]), ALU.mult))
            L(v.tensor_copy(smf, wideh(1)[:, :, 0:NS]))
            L(v.tensor_copy(smk, wideh(2)[:, :, 0:NS]))
            L.tell(v.tensor_copy(smq, group(Q_)[:, :, 0:NS]), "a_fg")
            dve.wait_ge(*mark["cum_done"])
            L(v.tensor_copy(Gt, bank(3)[0:TP, 0:12].rearrange("p (i h) -> p i h", i=NI)))
            L.tell(v.tensor_copy(Gl, bank(3)[0:TP, 16:28].rearrange("p (i h) -> p i h", i=NI)), "G_taken")
            L(tt(eGl, Gl, Gt, ALU.subtract))
            dve.wait_ge(sg["a_ln"], 1)
            for h in range(H):
                L(v.tensor_tensor_scan(wideh(1)[:, h, :], keep[:], proj[:, F_ + h, :], 0.0, ALU.mult, ALU.add))
            chunked = lambda a: a.rearrange("p (n t) -> p n t", t=C)
            NN = HT // C
            L.tell(tt(chunked(flat(F_)), chunked(W1), chunked(W1)[:, :, C // 2 - 1:C // 2].to_broadcast([128, NN, C]),
                      ALU.subtract), "a_diff")
            dve.wait_ge(sg["l2_root"], 1)
            L(stt(out=flat(QB_), in0=flat(QB_), scalar=SCALE, in1=cv[0], op0=ALU.mult, op1=ALU.mult))
            L.tell(v.tensor_copy(gmq, group(QB_)[:, :, 0:NS]), "b_normed", 1)
            dve.wait_ge(sg["l2_root"], 2)
            L(tt(flat(KB_), flat(KB_), cv[1], ALU.mult))
            L.tell(v.tensor_copy(gmk, group(KB_)[:, :, 0:NS]), "b_normed", 2)
            dve.wait_ge(sg["a_exp"], 2)
            L.tell(tt(W0, flat(Q_), W0, ALU.mult), "scA_ops", 1)
            L.tell(tt(flat(F_), W2, flat(F_), ALU.mult), "scA_ops", 2)
            dve.wait_ge(*mark["bcast_done"])
            dve.wait_ge(sg["G_exps"], 2)

            def chunk_cols(b0, c):
                a = ps[C * c:C * c + C, b0:b0 + NI, 0:H * TP].rearrange("p i (h t) -> p i h t", h=H)
                return a[:, :, :, C * c:C * c + C]

            for c in range(NCC):
                rows = slice(C * c, C * c + C)
                for i in range(NI):
                    ins = tt(LT[rows, i], chunk_cols(0, c)[:, i],
                             Gt[rows, i, :].rearrange("p (h o) -> p h o", o=1).to_broadcast([C, H, C]), ALU.subtract)
                    L(ins)
                dve.sem_inc(sg["G_diffs"], 1)
            L.tell(ts(LT, LT, 0.0, None, ALU.min), "lt_diff")
            dve.wait_ge(sg["a_expb"], 1)
            L(v.tensor_copy(decA, group(I_).rearrange("p h (n t) -> p h n t", t=C)[:, :, :, C - 1]))
            L(tt(flat(I_), flat(Q_), flat(I_), ALU.mult))
            L.tell(tt(chunked(flat(Q_)), chunked(W1)[:, :, C - 1:C].to_broadcast([128, NN, C]), chunked(W1), ALU.subtract),
                   "a_kdiff")
            dve.wait_ge(sg["vA_taken"], 1)
            L(v.memset(vtA[0:LEAD, 0], 0.0))
            bc = lambda m: m[:].rearrange("p (o t) -> p o t", o=1).to_broadcast([TP, NI * H, C])
            m12 = lambda a: a.rearrange("p i h t -> p (i h) t")
            dve.wait_ge(sg["lt_exp"], 3)
            L(tt(m12(LT), m12(LT), bc(causal), ALU.mult))
            L(tt(bG, bG, btm, ALU.mult))
            dve.wait_ge(sg["a_kexp"], 1)
            L.tell(tt(flat(Q_), W2, flat(Q_), ALU.mult), "kA_ready")
            dve.wait_ge(*mark["scA_done"])
            L.tell(tt(m12(PT), bank(3)[0:TP, 0:NI * H * C].rearrange("p (n t) -> p n t", t=C), bc(causal), ALU.mult),
                   "PT_ready")
            dve.wait_ge(*mark["scB_done"])
            prod = psf[0:TP, 0:768].rearrange("p (n t) -> p n t", t=2 * C)
            L(tt(m12(AT), prod[:, :, 0:C], m12(LT), ALU.mult))
            L(tt(m12(MT), prod[:, :, C:2 * C], m12(LT), ALU.mult))
            L(tt(m12(MT), m12(MT), bc(strict), ALU.mult))
            dve.wait_ge(*mark["beta_done"])
            L(v.tensor_copy(sbbeta, bank(3)[:, 0:H * TP].rearrange("p (h t) -> p h t", h=H)[:, :, 0:NS]))
            for c in range(NCC):
                rows = slice(C * c, C * c + C)
                for i in range(NI):
                    L(tt(MT[rows, i], chunk_cols(3, c)[:, i], MT[rows, i], ALU.mult))
            dve.sem_inc(mark["MT_ready"][0], 1)
            dve.wait_ge(sg["G_exps"], 1)
            L(v.tensor_copy(decB, cv[2].rearrange("p (h n t) -> p h n t", h=H, t=C)[:, :, :, C - 1]))
            L.tell(tt(flat(QB_), flat(QB_), cv[2], ALU.mult), "qdec_ready")
            heads = lambda b: bank(b)[0:TP, :].rearrange("p (h n) -> p h n", h=H)
            per_head = lambda a, i: a[:, i, :].rearrange("p (h o) -> p h o", o=1).to_broadcast([TP, H, DK])
            for i in range(NI):
                dve.wait_ge(sg["kB_turned"], i + 1)
                L(tt(kbe[:, i], heads(2 + i), per_head(bG, i), ALU.mult))
                L.tell(tt(kdB[:, i], heads(2 + i), per_head(eGl, i), ALU.mult), "kB_taken", i + 1)
            for i in range(NI):
                dve.wait_ge(sg["vB_turned"], i + 1)
                L.tell(tt(vb[:, i], heads((5, 0, 1)[i]), per_head(btm, i), ALU.mult), "vB_taken", i + 1)

            def write_state(b, spread, done, key, banks, base):
                dve.wait_ge(sg[spread], b + 1)
                for h in range(H):
                    stt(out=states[:, H * b + h, :], in0=bank(banks[b % 2])[:, 128 * h:128 * h + 128],
                        scalar=key[:, h, b:b + 1], in1=states[:, H * b + h, :], op0=ALU.mult, op1=ALU.add) \
                        .then_inc(sg[done], 1)
                dve.wait_ge(sg[done], H * b + H)
                dve.sem_inc(sg["spread_used"], 1)

            def update(S, dec, b, h, n, done):
                if n == 0:
                    v.tensor_copy(S[:, h, :], bank(b)[:, 128 * h:128 * h + 128]).then_inc(sg[done], 1)
                else:
                    stt(out=S[:, h, :], in0=S[:, h, :], scalar=dec[:, h, n:n + 1], in1=bank(b)[:, 128 * h:128 * h + 128],
                        op0=ALU.mult, op1=ALU.add).then_inc(sg[done], 1)

            dve.wait_ge(sg["stA_decayed"], 1)
            for b in range(NS):
                write_state(b, "stA_spread", "stA_new", smk, (2, 3), 0)
            dve.wait_ge(sg["pair_in"], 16)
            dve.wait_ge(sg["pairX_one"], 1)
            for k in range(2 * (C - 1)):
                j = k // 2
                n, m = j + 1, C - 1 - j
                wv = pairW[:, 0:n * m].rearrange("p (s t) -> p s t", s=n)
                if k:
                    dve.wait_ge(sg["solve_step"], k)
                if k % 2 == 0:
                    ins = tt(wv, pairX[:, 0:n, j:j + 1].to_broadcast([NP, n, m]), pairM[:, j:j + 1, j + 1:C]
                             .to_broadcast([NP, n, m]), ALU.mult)
                else:
                    ins = tt(pairX[:, 0:n, j + 1:C], pairX[:, 0:n, j + 1:C], wv, ALU.subtract)
                ins.then_inc(sg["solve_step"], 1)
                if k < H * NI * NCC:
                    n, h = k // H, k % H
                    if h == 0:
                        dve.wait_ge(sg["stepA_done"], n + 1)
                        if n:
                            dve.wait_ge(sg["stateA_upd"], H * n)
                    update(spA, decA, n % 2, h, n, "stateA_upd")
            dve.wait_ge(sg["solve_step"], 2 * (C - 1))
            dve.sem_inc(mark["inv_ready"][0], 1)

            def gated(out, root, o, w, g):
                dve.wait_ge(sg["n_root"], g + 1)
                dve.wait_ge(sg["silu_done"], g + 1)
                L(tt(flat(out), flat(out), root, ALU.mult))
                L.tell(stt(out=flat(out), in0=flat(out), scalar=prmT[:, w:w + 1], in1=flat(o), op0=ALU.mult, op1=ALU.mult),
                       "ya_ready", g + 1)

            gated(G_, flat(I_), Q_, 64, 0)
            dve.wait_ge(*mark["stB_kS"])
            L(tt(sdelta, proj[:, VB_:VB_ + H, 0:NS], bank(7)[:, 0:H * NS].rearrange("p (h b) -> p h b", h=H), ALU.subtract))
            L.tell(tt(sdelta, sdelta, sbbeta, ALU.mult), "stB_delta")
            for n in range(NI * NCC):
                dve.wait_ge(sg["kvB_done"], n + 1)
                if n:
                    dve.wait_ge(sg["stateB_upd"], H * n)
                for h in range(H):
                    update(spB, decB, 1 + n % 2, h, n, "stateB_upd")
                if n < NS:
                    write_state(n, "stB_spread", "stB_new", gmk, (3, 3), NS)
                if n:
                    dve.wait_ge(sg["gates_sig"], 1)
                    dve.wait_ge(sg["oa_done"], n)
                    tt(proj[:, GA_ + n - 1, :], bank(5)[:, 0:T], proj[:, GA_ + n - 1, :], ALU.mult) \
                        .then_inc(sg["oa_gated"], 1)
            gated(Z_, W1, KB_, 65, 1)
            dve.wait_ge(sg["gates_sig"], 2)
            dve.wait_ge(sg["oa_gated"], KT)
            for m in range(KT):
                t0 = proj[:, VB_ + m % 2, :]
                dve.wait_ge(sg["oab_done"], m + 1)
                L(tt(t0, bank(m)[:, 0:T], proj[:, GB_ + m, :], ALU.mult))
                L.tell(tt(feat[:, m, :], t0, proj[:, GA_ + m, :], ALU.add), "merged_ready", m + 1)
            dve.wait_ge(sg["route_consts"], 1)
            for i in range(NI):
                if i < 2:
                    dve.wait_ge(sg["b3_ready"], i + 1)
                    L.tell(stt(out=b_f32, in0=b3, scalar=lower[:, i:i + 1], in1=b_f32, op0=ALU.mult, op1=ALU.add),
                           "b3_less", i + 1)
                for j in range(2):
                    dve.wait_ge(sg["mix_done"], 2 * i + j + 1)
                    L.tell(tt(x_tok[:, i, 512 * j:512 * j + 512], x_tok[:, i, 512 * j:512 * j + 512],
                              bank(2 * i + j)[0:TP, :], ALU.add), "x2_ready", 2 * i + j + 1)
            dve.wait_ge(sg["nffn_in"], 16)
            for i in range(NI):
                dve.wait_ge(sg["x2_summed"], i + 1)
                L(v.reciprocal(rstd[:, i:i + 1], rstd[:, i:i + 1]))
                L.tell(stt(out=x2h[:, i, :], in0=x_tok[:, i, :], scalar=rstd[:, i:i + 1], in1=nffn_b,
                           op0=ALU.mult, op1=ALU.mult), "x2_normed", i + 1)
            dve.wait_ge(*mark["logits_done"])
            dve.wait_ge(sg["route_in"], 32)
            dve.wait_ge(sg["route_consts"], 1)
            L(tt(lg, bank(4)[0:TP, 0:NI * NE].rearrange("p (i e) -> p i e", i=NI),
                 br_b.rearrange("p (o e) -> p o e", o=1).to_broadcast([TP, NI, NE]), ALU.add))
            for i in range(NI):
                L(v.max(m8[:, i, :], lg[:, i, :]))
                L(v.max_index(i8[:, i, :], m8[:, i, :], lg[:, i, :]))
            L(v.tensor_copy(i8f, i8))
            for i in range(NI):
                L(tt(oneh[:, i], iota_e.rearrange("p (o e) -> p o e", o=1).to_broadcast([TP, TOP_K, NE]),
                     i8f[:, i, 0:TOP_K].rearrange("p (j o) -> p j o", o=1).to_broadcast([TP, TOP_K, NE]), ALU.is_equal))
            L(v.tensor_reduce(selm, oneh.rearrange("p i j e -> p i e j"), AX.X, ALU.add))
            L(tt(gate, m8[:, :, 0:TOP_K], m8[:, :, 0:1].to_broadcast([TP, NI, TOP_K]), ALU.subtract))
            L(ts(dump, dump, hole, None, ALU.mult))
            L(ts(hole, hole, -1.0, 1.0, ALU.mult, ALU.add))
            L(ts(oneh[:, 0], oneh[:, 0], hole, None, ALU.mult))
            L.tell(ts(selm[:, 0, :], selm[:, 0, :], hole, None, ALU.mult), "sel_done")
            dve.wait_ge(*mark["cnt_done"])
            cnt_c, ext = extc[:, 1:2], extc[:, 0:1]
            L(v.tensor_copy(cnt_c, bank(6)[0:NE, 0:1]))
            L(ts(ext, cnt_c, float(CAP), None, ALU.is_gt))
            n = 2 * CAP
            while n < T:
                L(ts(sel4[0:NE, 0:1], cnt_c, float(n), None, ALU.is_gt))
                L(tt(ext, ext, sel4[0:NE, 0:1], ALU.add))
                n += CAP
            dve.sem_inc(mark["ext_ready"][0], 1)
            dve.wait_ge(*mark["off_done"])
            L(v.tensor_copy(offc[:, 0:1], bank(6)[0:NE, 8:9]))
            L(tt(offc[:, 1:2], offc[:, 0:1], ext, ALU.add))
            L(ts(nblk, bank(6)[0:1, 16:17], float(NE), None, ALU.add))
            L(v.tensor_copy(nbi, nblk))
            L(ts(offx, bank(6)[0:TP, 64:64 + NE], float(NE - 1), None, ALU.add))
            L(tt(offx, offx, iota_e, ALU.subtract))
            L(v.tensor_copy(slot, bank(5)[0:TP, 0:NI * NE].rearrange("p (i e) -> p i e", i=NI)))
            L(ts(rtmp, slot, float(CAP), None, ALU.is_ge))
            over_tiles = lambda a: a.rearrange("p (o e) -> p o e", o=1).to_broadcast([TP, NI, NE])
            L(tt(rtmp, rtmp, over_tiles(offx), ALU.mult))
            L(tt(rtmp, rtmp, over_tiles(iota_e), ALU.add))
            L(stt(out=slot, in0=rtmp, scalar=float(CAP), in1=slot, op0=ALU.mult, op1=ALU.add))
            for i in range(NI):
                L(tt(oneh[:, i], oneh[:, i], slot[:, i:i + 1, :].to_broadcast([TP, TOP_K, NE]), ALU.mult))
            L(v.tensor_reduce(slotf, oneh, AX.X, ALU.add))
            L(v.tensor_copy(sloti, slotf))
            for j in range(TOP_K):
                L(ts(slotf[:, 0, j:j + 1], slotf[:, 0, j:j + 1], dump[:, j:j + 1], None, ALU.add))
            L.tell(v.tensor_copy(slotw, slotf), "slot_ready")
            L(ts(eh, iota_b, iota_p, None, ALU.is_equal))
            L(ts(iota_b, iota_b, -float(NE), None, ALU.add))
            L(ts(ehx, iota_b, offc[:, 0:1], None, ALU.is_ge))
            L(ts(iota_b, iota_b, offc[:, 1:2], None, ALU.is_lt))
            L(tt(ehx, ehx, iota_b, ALU.mult))
            L(tt(eh, eh, ehx, ALU.add))
            for p in range(2):
                L(v.tensor_copy(eh3[NE * p:NE * p + NE], eh))
            L.tell(v.tensor_copy(eh3[2 * NE:3 * NE], eh), "eh_ready")
            dve.wait_ge(sg["top_exp"], 1)
            L(v.tensor_reduce(gsum, gate, AX.X, ALU.add))
            L(v.reciprocal(gsum, gsum))
            L(tt(gate, gate, gsum.rearrange("p (i o) -> p i o", o=1).to_broadcast([TP, NI, TOP_K]), ALU.mult))
            dve.wait_ge(*mark["blk_done"])
            L(v.tensor_copy(blke, bank(6)[0:1, 128:128 + NBT]))
            dve.sem_inc(mark["nb_ready"][0], 1)
            dve.wait_ge(*mark["tok_turned"])
            L.tell(v.tensor_copy(tokT, bank(7)[0:CAP, 0:NBT]), "tokT_ready")
            dve.wait_ge(*mark["nb_ready"])
            nb = dve.value_load(nbi[0:1, 0:1], min_val=NE, max_val=NBX)
            rows_T = bank(2).rearrange("p (k t) -> p k t", k=KT)
            dve.wait_ge(sg["xg_turned"], 1)
            v.tensor_copy(xgT, rows_T).then_inc(sg["xg_ready"], 1)
            dve.sem_inc(sg["up_clipped"], 1)
            with dve.Fori(0, nb) as b:
                dve.wait_ge(sg["gu_used"], KT * b + KT)
                ts(hid_g, bank(0), SWIGLU_LIMIT, None, ALU.min).then_inc(sg["gate_clipped"], 1)
                ts(hid_u, bank(1), SWIGLU_LIMIT, -SWIGLU_LIMIT, ALU.min, ALU.max).then_inc(sg["up_clipped"], 1)
                dve.wait_ge(sg["gate_clipped"], b + 1)
                dve.wait_ge(sg["up_clipped"], b + 2)
                stt(out=hid_u, in0=hid_u, scalar=1.0, in1=hid_g, op0=ALU.add, op1=ALU.mult).then_inc(sg["gu_mult"], 1)
                dve.wait_ge(sg["gu_mult"], b + 1)
                dve.wait_ge(sg["sig_ready"], b + 1)
                tt(hid, hid_u, hid_s, ALU.mult).then_inc(sg["hid_ready"], 1)
                dve.wait_ge(sg["xg_turned"], b + 2)
                v.tensor_copy(xgT, rows_T).then_inc(sg["xg_ready"], 1)
            for i in range(NI):
                dve.wait_ge(sg[f"yg_in{i}"], 16 * TOP_K)
                for j in range(TOP_K):
                    L(stt(out=x_tok[:, i, :], in0=y_rows[i][j], scalar=gate[:, i, j:j + 1], in1=x_tok[:, i, :],
                          op0=ALU.mult, op1=ALU.add))
                dve.sem_inc(sg["yg_summed"], 1)
            dve.wait_ge(sg["nfin_in"], 16)
            for i in range(NI):
                dve.wait_ge(sg["f_summed"], i + 1)
                L(v.reciprocal(rstd[:, i:i + 1], rstd[:, i:i + 1]))
                L.tell(stt(out=x_tok[:, i, :], in0=x_tok[:, i, :], scalar=rstd[:, i:i + 1], in1=nfin_b,
                           op0=ALU.mult, op1=ALU.mult), "f_ready", i + 1)


_INS = ["x_prompt", "x_sample", "state_hgrn", "state_gdn", "state_conv", "meta_tokens", "lb_param", "norm_mix",
        "w_in", "conv_w", "a_log", "dt_bias", "hgrn_norm_w", "gdn_norm_w", "w_oa", "w_ob", "w_out", "norm_ffn",
        "w_router", "b_router", "w_gu", "b_gu", "w_down", "b_down", "norm_final"]


def kernel(**inputs):
    import numpy as _np
    import concourse.bacc as _bacc
    from concourse import mybir as _mybir
    from concourse.bass_utils import run_bass_kernel_spmd as _run

    nc = _bacc.Bacc("TRN2", target_bir_lowering=False, num_devices=1)
    arrays, args = {}, []
    for name in _INS:
        a = _np.ascontiguousarray(inputs[name])
        arrays[f"in_{name}"] = a
        args.append(nc.dram_tensor(f"in_{name}", a.shape, _mybir.dt.from_np(a.dtype), kind="ExternalInput").ap())
    shape = {n: inputs[n].shape for n in _INS}
    batch = shape["x_prompt"][0]
    outs = [shape["x_prompt"], shape["x_sample"],
            (shape["state_hgrn"][0], batch) + tuple(shape["state_hgrn"][2:]),
            (shape["state_gdn"][0], batch) + tuple(shape["state_gdn"][2:]),
            (shape["state_conv"][0], batch) + tuple(shape["state_conv"][2:]),
            shape["state_hgrn"], shape["state_gdn"], shape["state_conv"]]
    for i, s in enumerate(outs):
        args.append(nc.dram_tensor(f"out_{i}", tuple(s), _mybir.dt.float32, kind="ExternalOutput").ap())
    hybrid_decoder_step(nc, *args)
    r = _run(nc, [arrays], core_ids=[0])
    return tuple(r.results[0][f"out_{i}"] for i in range(len(outs)))
```
